# Optimizing a Trainium2 kernel written in Bass

```python
import math
import jax, jax.numpy as jnp
from jax import lax
import numpy as np

D_MODEL = 1024
BATCH = 1
SEQ = 512
DEPTH = 1
DEC_BATCH = 8
DEC_SEQ = 4
PAST_LEN = 4096
PAGE_SIZE = 128

DN_HEADS = 8
DN_HEAD_DIM = 128
DN_WIDTH = DN_HEADS * DN_HEAD_DIM
QKV_WIDTH = 3 * DN_WIDTH
CONV_WIDTH = 4
DN_CHUNK = 64
POOL_WINDOWS = (2, 4, 8, 16)
POOL_GROUPS = len(POOL_WINDOWS)
POOL_GROUP_DIM = 128
POOL_WIDTH = POOL_GROUPS * POOL_GROUP_DIM
POOL_OUT_GROUP = D_MODEL // POOL_GROUPS
POOL_BUF = max(POOL_WINDOWS) - 1
IN_WIDTH = QKV_WIDTH + 2 * DN_HEADS + DN_WIDTH + POOL_WIDTH + 2 * D_MODEL
PEER_HEADS = 8
PEER_NKEYS = 128
PEER_EXPERTS = PEER_NKEYS * PEER_NKEYS
PEER_TOPK = 16
PEER_KEY_HALF = 128
PEER_TOKEN_BLOCK = 512
EPS = 1e-6

kernel_name = 'hybrid_deltanet_pool_peer_adaln_step'

def rmsnorm(x, g):
    xf = x.astype(jnp.float32)
    y = xf * lax.rsqrt(jnp.mean(xf * xf, axis=-1, keepdims=True) + EPS)
    return (y * g.astype(jnp.float32)).astype(x.dtype)

def l2norm(x):
    return x * lax.rsqrt(jnp.sum(x * x, axis=-1, keepdims=True) + EPS)

def short_conv(x, buf, w):
    L = x.shape[1]
    xp = jnp.concatenate([buf.astype(x.dtype), x], axis=1)
    y = sum(xp[:, k:k + L] * w[k] for k in range(CONV_WIDTH))
    return jax.nn.silu(y), xp[:, L:]

def gated_delta_rule(q, k, v, g, beta, s0):
    f32 = jnp.float32
    B, L, H, Dk = q.shape
    Dv = v.shape[-1]
    C = L if L <= DN_CHUNK else math.gcd(L, DN_CHUNK)
    N = L // C

    def to_chunks(t):
        t = jnp.moveaxis(t.astype(f32), 2, 1)
        return t.reshape((B, H, N, C) + t.shape[3:])

    q, k, v, g, beta = [to_chunks(t) for t in (q, k, v, g, beta)]
    q = q * (Dk ** -0.5)
    g = jnp.cumsum(g, axis=-1)
    k_beta = k * beta[..., None]
    v_beta = v * beta[..., None]
    idx = jnp.arange(C)
    causal = idx[:, None] >= idx[None, :]
    strict = idx[:, None] > idx[None, :]
    decay = jnp.exp(jnp.where(causal, g[..., :, None] - g[..., None, :], -jnp.inf))
    lower = jnp.einsum('bhnid,bhnjd->bhnij', k_beta, k) * decay * strict
    a_mat = lower + jnp.eye(C, dtype=f32)
    rhs = jnp.concatenate([v_beta, k_beta * jnp.exp(g)[..., None]], axis=-1)
    sol = lax.linalg.triangular_solve(a_mat, rhs, left_side=True, lower=True, unit_diagonal=True)
    u, w = sol[..., :Dv], sol[..., Dv:]
    qk = jnp.einsum('bhnid,bhnjd->bhnij', q, k) * decay
    g_last = g[..., -1]
    k_tail = k * jnp.exp(g_last[..., None] - g)[..., None]
    xs = tuple(jnp.moveaxis(t, 2, 0) for t in (q, qk, u, w, g, g_last, k_tail))

    def step(S, inp):
        q_c, qk_c, u_c, w_c, g_c, gl_c, kt_c = inp
        v_new = u_c - jnp.einsum('bhck,bhkv->bhcv', w_c, S)
        o = (jnp.einsum('bhck,bhkv->bhcv', q_c * jnp.exp(g_c)[..., None], S)
             + jnp.einsum('bhij,bhjv->bhiv', qk_c, v_new))
        S = S * jnp.exp(gl_c)[..., None, None] + jnp.einsum('bhck,bhcv->bhkv', kt_c, v_new)
        return S, o

    S, o = lax.scan(step, s0.astype(f32), xs)
    o = jnp.moveaxis(o, 0, 2).reshape(B, H, L, Dv)
    return jnp.moveaxis(o, 1, 2), S

def deltanet_branch(qkv_raw, b_raw, a_raw, z, conv_buf, s0, conv_w, a_log, dt_bias, dn_norm_g):
    f32 = jnp.float32
    B, L, _ = qkv_raw.shape
    qkv, new_conv = short_conv(qkv_raw, conv_buf, conv_w)
    qkv = qkv.astype(f32).reshape(B, L, 3, DN_HEADS, DN_HEAD_DIM)
    q = l2norm(qkv[:, :, 0])
    k = l2norm(qkv[:, :, 1])
    v = qkv[:, :, 2]
    beta = jax.nn.sigmoid(b_raw.astype(f32))
    g = -jnp.exp(a_log.astype(f32)) * jax.nn.softplus(a_raw.astype(f32) + dt_bias.astype(f32))
    o, s_new = gated_delta_rule(q, k, v, g, beta, s0)
    zf = z.astype(f32).reshape(B, L, DN_HEADS, DN_HEAD_DIM)
    o = (o * lax.rsqrt(jnp.mean(o * o, axis=-1, keepdims=True) + EPS)
         * dn_norm_g.astype(f32) * jax.nn.silu(zf))
    return o.reshape(B, L, DN_WIDTH).astype(qkv_raw.dtype), new_conv, s_new.astype(s0.dtype)

def pool_branch(p_in, buf, start, w_pool, pool_scale):
    f32 = jnp.float32
    B, L, _ = p_in.shape
    xf = p_in.astype(f32)
    seq = jnp.concatenate([buf.astype(f32), xf], axis=1)
    cs = jnp.concatenate([jnp.zeros((B, 1, POOL_WIDTH), f32), jnp.cumsum(seq, axis=1)], axis=1)
    top = cs[:, POOL_BUF + 1:POOL_BUF + 1 + L]
    pos = start + jnp.arange(L)
    means = []
    for gi, win in enumerate(POOL_WINDOWS):
        lo, hi = gi * POOL_GROUP_DIM, (gi + 1) * POOL_GROUP_DIM
        s = top[..., lo:hi] - cs[:, POOL_BUF + 1 - win:POOL_BUF + 1 - win + L, lo:hi]
        cnt = jnp.minimum(pos + 1, win).astype(f32)
        means.append(s / cnt[None, :, None])
    pooled = (jnp.concatenate(means, axis=-1) - xf).reshape(B, L, POOL_GROUPS, POOL_GROUP_DIM)
    y = jnp.einsum('blgc,gco->blgo', pooled, w_pool.astype(f32)).reshape(B, L, D_MODEL)
    y = y * pool_scale.astype(f32)
    return y.astype(p_in.dtype), seq[:, -POOL_BUF:].astype(buf.dtype)

def peer(h, w_query, sub_keys, expert_u, expert_v):
    f32 = jnp.float32
    B, L, D = h.shape
    T = B * L
    x = h.reshape(T, D)
    q = (x @ w_query).astype(f32).reshape(T, PEER_HEADS, 2, PEER_KEY_HALF)
    scores = jnp.einsum('thpd,hpnd->thpn', q, sub_keys.astype(f32))
    s_top, i_top = lax.top_k(scores, PEER_TOPK)
    cand = s_top[:, :, 0, :, None] + s_top[:, :, 1, None, :]
    cand_idx = i_top[:, :, 0, :, None] * PEER_NKEYS + i_top[:, :, 1, None, :]
    best, sel = lax.top_k(cand.reshape(T, PEER_HEADS, PEER_TOPK * PEER_TOPK), PEER_TOPK)
    idx = jnp.take_along_axis(cand_idx.reshape(T, PEER_HEADS, PEER_TOPK * PEER_TOPK), sel, axis=-1)
    gates = jax.nn.softmax(best, axis=-1)
    HK = PEER_HEADS * PEER_TOPK
    nb = T if T <= PEER_TOKEN_BLOCK else math.gcd(T, PEER_TOKEN_BLOCK)

    def token_block(args):
        xb, ib, gb = args
        act = jax.nn.gelu(jnp.einsum('td,tkd->tk', xb, expert_u[ib]).astype(f32), approximate=False)
        coef = (gb * act).astype(xb.dtype)
        return jnp.einsum('tk,tkd->td', coef, expert_v[ib])

    out = lax.map(token_block, (x.reshape(T // nb, nb, D),
                                idx.reshape(T // nb, nb, HK),
                                gates.reshape(T // nb, nb, HK)))
    return out.reshape(B, L, D).astype(h.dtype)

def trunk_layer(x, c, conv_buf, s0, pool_buf, start,
                w_ada, b_ada, norm1_g, w_in, conv_w, a_log, dt_bias, dn_norm_g,
                w_pool, pool_scale, w_out, norm2_g, w_query, sub_keys, expert_u, expert_v):
    B = x.shape[0]
    mod = (jax.nn.silu(c) @ w_ada + b_ada).reshape(B, 6, D_MODEL)[:, :, None, :]
    sh1, sc1, g1, sh2, sc2, g2 = [mod[:, i] for i in range(6)]
    h = rmsnorm(x, norm1_g) * (1 + sc1) + sh1
    proj = h @ w_in
    widths = (QKV_WIDTH, DN_HEADS, DN_HEADS, DN_WIDTH, POOL_WIDTH, D_MODEL, D_MODEL)
    offs = [int(o) for o in np.cumsum(widths)[:-1]]
    qkv_raw, b_raw, a_raw, z, pool_in, gate_a, gate_b = jnp.split(proj, offs, axis=-1)
    o_dn, new_conv, new_s = deltanet_branch(qkv_raw, b_raw, a_raw, z, conv_buf, s0,
                                            conv_w, a_log, dt_bias, dn_norm_g)
    o_pool, new_pool = pool_branch(pool_in, pool_buf, start, w_pool, pool_scale)
    mixed = jax.nn.sigmoid(gate_a) * o_dn + jax.nn.sigmoid(gate_b) * o_pool
    x = x + g1 * (mixed @ w_out)
    h2 = rmsnorm(x, norm2_g) * (1 + sc2) + sh2
    x = x + g2 * peer(h2, w_query, sub_keys, expert_u, expert_v)
    return x, new_conv, new_s, new_pool

def setup_inputs(seed: int = 0) -> dict:
    key = jax.random.key(seed)
    ks = jax.random.split(key, 24)
    f32 = jnp.float32
    D = D_MODEL

    def nrm(k, shape, s):
        return jax.random.normal(k, shape, f32) * s

    return {
        'x_prompt': nrm(ks[0], (BATCH, SEQ, D), 1.0),
        'x_sample': nrm(ks[1], (DEC_BATCH, DEC_SEQ, D), 1.0),
        'c_prompt': nrm(ks[2], (BATCH, D), 1.0),
        'c_sample': nrm(ks[3], (DEC_BATCH, D), 1.0),
        'state_conv': nrm(ks[4], (DEPTH, DEC_BATCH, CONV_WIDTH - 1, QKV_WIDTH), 1.0),
        'state_delta': nrm(ks[5], (DEPTH, DEC_BATCH, DN_HEADS, DN_HEAD_DIM, DN_HEAD_DIM), 0.05),
        'state_pool': nrm(ks[6], (DEPTH, DEC_BATCH, POOL_BUF, POOL_WIDTH), 1.0),
        'w_ada': nrm(ks[7], (DEPTH, D, 6 * D), 0.5 * D ** -0.5),
        'b_ada': nrm(ks[8], (DEPTH, 6 * D), 0.02),
        'norm1_g': 1.0 + nrm(ks[9], (DEPTH, D), 0.02),
        'w_in': nrm(ks[10], (DEPTH, D, IN_WIDTH), D ** -0.5),
        'conv_w': nrm(ks[11], (DEPTH, CONV_WIDTH, QKV_WIDTH), CONV_WIDTH ** -0.5),
        'a_log': jnp.log(jax.random.uniform(ks[12], (DEPTH, DN_HEADS), f32, 1.0, 8.0)),
        'dt_bias': nrm(ks[13], (DEPTH, DN_HEADS), 0.1),
        'dn_norm_g': 1.0 + nrm(ks[14], (DEPTH, DN_HEAD_DIM), 0.02),
        'w_pool': nrm(ks[15], (DEPTH, POOL_GROUPS, POOL_GROUP_DIM, POOL_OUT_GROUP), POOL_GROUP_DIM ** -0.5),
        'pool_scale': 1.0 + nrm(ks[16], (DEPTH, D), 0.1),
        'w_out': nrm(ks[17], (DEPTH, D, D), D ** -0.5),
        'norm2_g': 1.0 + nrm(ks[18], (DEPTH, D), 0.02),
        'w_query': nrm(ks[19], (DEPTH, D, PEER_HEADS * 2 * PEER_KEY_HALF), D ** -0.5),
        'sub_keys': nrm(ks[20], (DEPTH, PEER_HEADS, 2, PEER_NKEYS, PEER_KEY_HALF), PEER_KEY_HALF ** -0.5),
        'expert_u': nrm(ks[21], (DEPTH, PEER_EXPERTS, D), D ** -0.5),
        'expert_v': nrm(ks[22], (DEPTH, PEER_EXPERTS, D), 0.5),
        'final_norm_g': 1.0 + nrm(ks[23], (D,), 0.02),
    }

def reference(x_prompt, x_sample, c_prompt, c_sample, state_conv, state_delta, state_pool,
              w_ada, b_ada, norm1_g, w_in, conv_w, a_log, dt_bias, dn_norm_g,
              w_pool, pool_scale, w_out, norm2_g, w_query, sub_keys, expert_u, expert_v,
              final_norm_g):
    bp = x_prompt.shape[0]
    dt = x_prompt.dtype
    zero_conv = jnp.zeros((bp, CONV_WIDTH - 1, QKV_WIDTH), dt)
    zero_delta = jnp.zeros((bp, DN_HEADS, DN_HEAD_DIM, DN_HEAD_DIM), state_delta.dtype)
    zero_pool = jnp.zeros((bp, POOL_BUF, POOL_WIDTH), dt)
    yp, ys = x_prompt, x_sample
    conv_p, delta_p, pool_p, conv_s, delta_s, pool_s = [], [], [], [], [], []
    for layer in range(DEPTH):
        wl = (w_ada[layer], b_ada[layer], norm1_g[layer], w_in[layer], conv_w[layer],
              a_log[layer], dt_bias[layer], dn_norm_g[layer], w_pool[layer], pool_scale[layer],
              w_out[layer], norm2_g[layer], w_query[layer], sub_keys[layer],
              expert_u[layer], expert_v[layer])
        yp, cp, sp, pp = trunk_layer(yp, c_prompt, zero_conv, zero_delta, zero_pool, 0, *wl)
        ys, cs, ss, ps = trunk_layer(ys, c_sample, state_conv[layer], state_delta[layer],
                                     state_pool[layer], PAST_LEN, *wl)
        conv_p.append(cp)
        delta_p.append(sp)
        pool_p.append(pp)
        conv_s.append(cs)
        delta_s.append(ss)
        pool_s.append(ps)
    y_prompt = rmsnorm(yp, final_norm_g)
    y_sample = rmsnorm(ys, final_norm_g)
    return (y_prompt, y_sample,
            jnp.stack(conv_p), jnp.stack(delta_p), jnp.stack(pool_p),
            jnp.stack(conv_s), jnp.stack(delta_s), jnp.stack(pool_s))


_drawn_inputs = setup_inputs


def setup_inputs(seed=0):
    import zlib

    import numpy as np

    out = dict(_drawn_inputs(seed))
    spreads = {}
    factors = {'state_delta': 3.396,
     'dt_bias': 3.33,
     'dn_norm_g': 8.0,
     'pool_scale': 2.94,
     'norm2_g': 4.54,
     'final_norm_g': 2.91}
    for name, (base, spread) in spreads.items():
        noise = np.random.default_rng([zlib.crc32(name.encode()), seed]).standard_normal(out[name].shape)
        drawn = base * np.exp(spread * noise) if base else spread * noise
        out[name] = __import__('jax').numpy.asarray(drawn.astype(out[name].dtype))
    for name, factor in factors.items():
        out[name] = (out[name] * factor).astype(out[name].dtype)
    return out
```

```python
from contextlib import ExitStack

import numpy as np

import concourse.bass as bass
from concourse import mybir

F32 = mybir.dt.float32
F32R = mybir.dt.float32r
U32 = mybir.dt.uint32
ALU = mybir.AluOpType
ACT = mybir.ActivationFunctionType
AX_X = mybir.AxisListType.X

P = 128
D = 1024
KC = D // P
TP = 512
NSEQ, LS = 8, 4
TS = NSEQ * LS
NT = TP + TS
HN = NT // 2
NG = 1 + NSEQ
H = 8
CW = 4
NC = TP // P
TT = NC + 1
WINDOWS = (2, 4, 8, 16)
PB_ = 15
SEG_C = CW - 1 + LS
CB = CW - 1 + TP + NSEQ * SEG_C
CY = CB - (CW - 1)
CS0 = TP + CW - 1
SEG_P = PB_ + LS
PBW = PB_ + TP + NSEQ * SEG_P
PS0 = PB_ + TP
EPS = 1e-6
NEXP = 128
TOPK = 16
LOG_EXP_SET = 6

N_Z, N_GA, N_POOL, N_GB = 8, 8, 4, 8
C_Z = 0
C_GA = C_Z + N_Z
C_POOL = C_GA + N_GA
C_GB = C_POOL + N_POOL
C_QKV = C_GB + N_GB
C_OUT = C_QKV + 3 * H
C_QUERY = C_OUT + KC
C_U = C_QUERY + 2 * H
N_STREAM = C_U + NEXP
LASTING = {"w_landed0", "w_landed1", "w_hi_done", "w_lo_done", "pp_done0", "pp_done1", "pp_read0", "pp_read1",
           "act_gate", "dve_gate", "pool_gate", "out_st", "s_ld"}

JG = 4
NGRP = NEXP // JG
TB = 32
NTB = NT // TB
NLV = 6
HOTS = 4

VEC = {}
_at = 0
for _name, _n in (("g1", 8), ("g2", 8), ("gf", 8), ("pool_scale", 8), ("b_ada", 48), ("dn_g", 1),
                  ("conv_w", 96), ("dt", 8), ("a_log", 8)):
    VEC[_name] = (_at, _at + _n)
    _at += _n
NVEC = _at
CST = {}
_at = 0
for _name, _n in (("ident", 128), ("ones", 128), ("ut", 128), ("levels", 7 * 128), ("uts", 32),
                  ("bds", 32), ("iota", 128), ("rc", 64), ("iota16", 16), ("seqmask", 8)):
    CST[_name] = (_at, _at + _n)
    _at += _n
NCST = _at
SH1, SC1, G1, SH2, SC2, G2 = (KC * n for n in range(6))
N_ADA = 6 * KC // 4
N_ADA1 = 2 * KC // 4


def constants():
    c = np.zeros((P, NCST), np.float32)

    def put(name, a):
        lo, _ = CST[name]
        c[:a.shape[0], lo:lo + a.shape[1]] = a

    r = np.arange(P)
    put("ident", np.eye(P))
    put("ones", np.ones((P, P)))
    put("ut", r[:, None] <= r[None, :])
    levels = []
    for n in range(7):
        s = 1 << n
        same = r[:, None] // (2 * s) == r[None, :] // (2 * s)
        levels.append(same & (r[:, None] % (2 * s) < s) & (r[None, :] % (2 * s) >= s))
    put("levels", np.concatenate(levels, 1))
    t = np.arange(TS)
    same = t[:, None] // LS == t[None, :] // LS
    put("uts", same & (t[:, None] <= t[None, :]))
    put("bds", same)
    put("iota", np.tile(r, (P, 1)))
    put("rc", np.tile(np.concatenate([1.0 / np.minimum(np.arange(16) + 1, w) for w in WINDOWS]), (P, 1)))
    put("iota16", np.tile(np.arange(16), (P, 1)))
    put("seqmask", t[:, None] // LS == np.arange(NSEQ)[None, :])
    return c


class Chunk:

    def __init__(self, base, off=0, per=0, i=0):
        k = base + off
        self.slot = k % 2
        self.turn = (k // 2) if per == 0 else i * (per // 2) + (k // 2)
        self.n = k if per == 0 else i * per + k
        self.make = lambda d: Chunk(base, off + d, per, i)

    def __add__(self, d):
        return self.make(d)


class Steps:

    def __init__(self, eng, sem, before=0):
        self.eng, self.sem, self.before, self.n = eng, sem, before, 0

    def __call__(self, ins):
        ins.then_inc(self.sem, 1)
        self.n += 1

    def settle(self):
        self.eng.wait_ge(self.sem, self.before + self.n)


def build(nc, x_in, c_in, vec_in, cst_in, wba_in, ada_in, stream_in, v_in, conv_in, pool_in, delta_in,
          wpool_in, keys_in, y_out, conv_out, delta_p_out, delta_s_out, pool_out):
    with ExitStack() as ctx:
        def sb(name, shape, dt=F32, stack=ctx):
            return stack.enter_context(nc.sbuf_tensor(name, shape, dt))

        names = set()

        def sem(name):
            assert name not in names
            names.add(name)
            lasting = name in LASTING
            s = nc.alloc_semaphore(name)
            if not lasting:
                phase_sems.append(s)
            return s

        def retire(pool, sems):
            nc.clear_and_free_semaphores(sems)

        phase_sems = []

        x = sb("x", [P, KC, NT])
        act_hi = sb("act_hi", [P, KC, NT], F32R)
        act_lo = sb("act_lo", [P, KC, NT], F32R)
        w_raw = [sb(f"w_raw{s}", [P, D]) for s in range(2)]
        w_hi = [sb(f"w_hi{s}", [P, D], F32R) for s in range(2)]
        w_lo = [sb(f"w_lo{s}", [P, D], F32R) for s in range(2)]
        vec = sb("vec", [P, NVEC])
        cst = sb("cst", [P, NCST])
        eps = sb("eps", [P, 1])
        one = sb("one", [P, 1])
        mod = sb("mod", [P, 6 * KC, NG])
        aff1 = sb("aff1", [P, KC, NG])
        aff2 = sb("aff2", [P, KC, NG])

        def v_(name):
            return vec[:, VEC[name][0]:VEC[name][1]]

        def c_(name, rows=P):
            return cst[0:rows, CST[name][0]:CST[name][1]]

        ident, ones, ut, iota = c_("ident"), c_("ones"), c_("ut"), c_("iota")

        def level(n, rows=P):
            lo = CST["levels"][0] + n * P
            return cst[0:rows, lo:lo + rows]

        ba = sb("ba", [P, TT, 2 * H])
        GRAW, BETA, GCUM, ETAIL, ETOT, NBEG = range(6)
        tok = sb("tok", [P, 6, TT, H])
        tmp_a = sb("tmp_a", [P, TT, H])
        tmp_b = sb("tmp_b", [P, TT, H])
        tmp_c = sb("tmp_c", [P, TT, H])
        ea_log = sb("ea_log", [P, H])

        with ExitStack() as st:
            ada_w = [sb(f"ada_w{s}", [P, KC, 4 * P], stack=st) for s in range(4)]
            ada_t = sb("ada_t", [NG, 4, 4 * P], stack=st)
            h1 = sb("h1", [P, KC, NT], stack=st)
            sq1 = sb("sq1", [P, KC, NT], stack=st)
            rstd1 = sb("rstd1", [P, NT], stack=st)
            c_raw = sb("c_raw", [P, KC, NG], stack=st)
            c_silu = sb("c_silu", [P, KC, NG], stack=st)
            wba = sb("wba", [P, KC, 2 * H], stack=st)
        with ExitStack() as st:
            zg = sb("zg", [P, KC, NT], stack=st)
            mixed = sb("mixed", [P, KC, NT], stack=st)
            qkv_s = sb("qkv_s", [P, H, 3, TS], stack=st)
            conv_st = sb("conv_st", [P, 3 * H, NSEQ, CW - 1], stack=st)
            conv_new = sb("conv_new", [P, 3 * H, NG, CW - 1], stack=st)
            s_fin = sb("s_fin", [P, H, P], stack=st)
            pool_new = sb("pool_new", [P, len(WINDOWS), NG, PB_], stack=st)
            with ExitStack() as st2:
                pool_st = sb("pool_st", [P, len(WINDOWS), NSEQ, PB_], stack=st2)
                pbuf = sb("pbuf", [P, len(WINDOWS), PBW], stack=st2)
                psum_w = [sb(f"psum_w{s}", [P, PBW], stack=st2) for s in range(2)]
                pooled = sb("pooled", [P, len(WINDOWS), NT], stack=st2)
                wpool = sb("wpool", [P, len(WINDOWS), 2 * P], stack=st2)
                sig = [sb(f"sig{s}", [P, NT], stack=st2) for s in range(2)]
            with ExitStack() as st2:
                cbuf = [sb(f"cbuf{s}", [P, CB], stack=st2) for s in range(2)]
                qkv_h = [sb(f"qkv_h{s}", [P, 3, CB], stack=st2) for s in range(2)]
                qk_sq = sb("qk_sq", [P, 2, CY], stack=st2)
                qk_rs = sb("qk_rs", [P, 2, CY], stack=st2)
                hs = sb("hs", [P, 6, TT], stack=st2)
                decay = sb("decay", [P, TP], stack=st2)
                eg_row = sb("eg_row", [P, TP], stack=st2)
                kb = sb("kb", [P, TP], stack=st2)
                qe = sb("qe", [P, TP], stack=st2)
                lt = sb("lt", [P, TP], stack=st2)
                lm = [sb(f"lm{s}", [P, TP], stack=st2) for s in range(2)]
                qk = sb("qk", [P, TP], stack=st2)
                tu = sb("tu", [P, TP], stack=st2)
                ti = sb("ti", [P, TP], stack=st2)
                ap_ = [sb(f"ap_{n}", [P, TP], stack=st2) for n in range(NLV)]
                k_tail = sb("k_tail", [P, TP], stack=st2)
                v_beta = sb("v_beta", [P, TP], stack=st2)
                v_new = sb("v_new", [P, TP], stack=st2)
                r_new = sb("r_new", [P, TP], stack=st2)
                s_run = sb("s_run", [P, 2, P], stack=st2)
                o_sq = sb("o_sq", [P, TP], stack=st2)
                o_rs = sb("o_rs", [P, TP], stack=st2)
                o_t = sb("o_t", [P, TP], stack=st2)
            with ExitStack() as st2:
                s_s = sb("s_s", [P, H, NSEQ, P], stack=st2)
                eg_s = sb("eg_s", [P, H, TS], stack=st2)
                kb_s = sb("kb_s", [P, H, TS], stack=st2)
                qe_s = sb("qe_s", [P, H, TS], stack=st2)
                ks_s = sb("ks_s", [P, H, TS], stack=st2)
                osq_s = sb("osq_s", [P, H, TS], stack=st2)
                ors_s = sb("ors_s", [P, H, TS], stack=st2)
                decay_s = sb("decay_s", [TS, H, TS], stack=st2)
                lt_s = sb("lt_s", [TS, H, TS], stack=st2)
                lm_s = sb("lm_s", [TS, H, TS], stack=st2)
                qk_s = sb("qk_s", [TS, H, TS], stack=st2)
                tu_s = sb("tu_s", [TS, H, TS], stack=st2)
                ti_s = sb("ti_s", [TS, H, TS], stack=st2)
                ap_s = sb("ap_s", [TS, H, TS], stack=st2)
                kt_s = sb("kt_s", [TS, H, P], stack=st2)
                vb_s = sb("vb_s", [TS, H, P], stack=st2)
                r_s = sb("r_s", [TS, H, P], stack=st2)
                vn_s = sb("vn_s", [TS, H, P], stack=st2)
                km_s = [sb(f"km_s{s}", [TS, NSEQ, P], stack=st2) for s in range(2)]
            h2 = sb("h2", [P, KC, NT], stack=st)
            sq2 = sb("sq2", [P, KC, NT], stack=st)
            rstd2 = sb("rstd2", [P, NT], stack=st)
            res_t = [sb(f"res_t{s}", [P, TS], stack=st) for s in range(2)]

        with ExitStack() as st:
            scores = sb("scores", [P, TT, 2 * H, P], stack=st)
            with ExitStack() as st2:
                keys = sb("keys", [P, 2 * H, P], stack=st2)
                qt = [sb(f"qt{s}", [P, NT], stack=st2) for s in range(2)]
            wk = sb("wk", [P, 2 * H, P], stack=st)
            wk2 = sb("wk2", [P, 2 * H, P], stack=st)
            top = sb("top", [P, 2 * H, TOPK], stack=st)
            top_i = sb("top_i", [P, 2 * H, TOPK], U32, stack=st)
            top_f = sb("top_f", [P, 2 * H, TOPK], stack=st)
            cand = sb("cand", [P, H, TOPK, TOPK], stack=st)
            best = sb("best", [P, H, TOPK], stack=st)
            sel = sb("sel", [P, H, TOPK], U32, stack=st)
            sel_ab = sb("sel_ab", [P, 2, H, TOPK], U32, stack=st)
            sel_f = sb("sel_f", [P, 2, H, TOPK], stack=st)
            trio = sb("trio", [P, 3, P], stack=st)
            gsum = sb("gsum", [P, H], stack=st)
            gcols = sb("gcols", [P, 3, P], stack=st)
            hot_a = sb("hot_a", [P, 4 * HOTS, P], stack=st)
            hot_b = sb("hot_b", [P, 4 * HOTS, P], stack=st)
            gstage = [sb(f"gstage{s}", [P, P, TB], stack=st) for s in range(2)]
        with ExitStack() as st:
            acc = sb("acc", [P, KC, NT], stack=st)
            with ExitStack() as st2:
                sq3 = sb("sq3", [P, KC, NT], stack=st2)
                rstd3 = sb("rstd3", [P, NT], stack=st2)
            v_raw = [sb(f"v_raw{s}", [P, D], stack=st) for s in range(2)]
            v_hi = [sb(f"v_hi{s}", [P, D], F32R, stack=st) for s in range(JG)]
            v_lo = [sb(f"v_lo{s}", [P, D], F32R, stack=st) for s in range(JG)]
            gt = sb("gt", [P, NTB, JG, TB], stack=st)
            ge = [sb(f"ge{s}", [P, NT], stack=st) for s in range(2)]
            cf = [sb(f"cf{s}", [P, NT], stack=st) for s in range(2)]
            co_hi = [sb(f"co_hi{s}", [P, NT], F32R, stack=st) for s in range(JG)]
            co_lo = [sb(f"co_lo{s}", [P, NT], F32R, stack=st) for s in range(JG)]

        gates_d = nc.dram_tensor("gate_matrix", (NTB, P, P, TB), F32, kind="Internal").ap()

        pp = [ctx.enter_context(nc.psum_tensor(f"pp{s}", [P, 2, 512], F32)) for s in range(2)]
        dd = ctx.enter_context(nc.psum_tensor("dd", [P, 4, 512], F32))

        def halves(t):
            return t.rearrange("p (b n) -> p b n", b=2)

        w_landed = [sem(f"w_landed{s}") for s in range(2)]
        w_hi_done = sem("w_hi_done")
        w_lo_done = sem("w_lo_done")
        pp_done = [sem(f"pp_done{s}") for s in range(2)]
        pp_read = [sem(f"pp_read{s}") for s in range(2)]
        act_gate = sem("act_gate")
        dve_gate = sem("dve_gate")
        pool_gate = sem("pool_gate")

        def gate_act(act, s, value):
            act.wait_ge(s, value)
            act.sem_inc(act_gate, 1)

        def gate_dve(dve, s, value):
            dve.wait_ge(s, value)
            dve.sem_inc(dve_gate, 1)

        def gate_pool(pool, s, value):
            pool.wait_ge(s, value)
            pool.sem_inc(pool_gate, 1)

        def load_chunk(sp, k):
            if not (isinstance(k.n, int) and k.n < 2):
                sp.wait_ge(w_lo_done, k.n - 1)
            n = k.n
            src = stream_in[bass.ds(n, 1)].rearrange("a p c -> p (a c)")
            sp.dma_start(w_raw[k.slot][:], src).then_inc(w_landed[k.slot], 16)

        def split_hi(act, k):
            act.wait_ge(w_landed[k.slot], 16 * k.turn + 16)
            act.wait_ge(pp_done[k.slot], k.turn + 1)
            nc.scalar.activation(w_hi[k.slot][:], w_raw[k.slot][:], ACT.Copy).then_inc(w_hi_done, 1)

        def split_lo(dve, k):
            dve.wait_ge(w_hi_done, k.n + 1)
            nc.vector.tensor_tensor(w_lo[k.slot][:], w_raw[k.slot][:], w_hi[k.slot][:].bitcast(F32),
                                    ALU.subtract).then_inc(w_lo_done, 1)

        def product(pe, k, part=range(KC)):
            s = k.slot
            if part[0] == 0:
                pe.wait_ge(w_lo_done, k.n + 1)
                pe.wait_ge(pp_read[s], k.turn + 1)
            for c in part:
                for w, a in ((w_hi[s], act_hi), (w_hi[s], act_lo), (w_lo[s], act_hi)):
                    for b in range(2):
                        last = nc.tensor.matmul(pp[s][:, b, 0:HN], w[:, c * P:(c + 1) * P],
                                                a[:, c, b * HN:(b + 1) * HN],
                                                start=(c == 0 and w is w_hi[s] and a is act_hi),
                                                stop=(c == KC - 1 and w is w_lo[s]))
            if part[-1] == KC - 1:
                last.then_inc(pp_done[s], 1)

        def done(eng, k):
            eng.wait_ge(pp_done[k.slot], k.turn + 2)

        def read(eng, k):
            eng.wait_ge(pp_read[k.slot], k.turn + 2)

        def sample_cols(t):
            return t[:, :, TP:NT].rearrange("p k (s t) -> p k s t", s=NSEQ)

        x_ld, small_ld = sem("x_ld"), sem("small_ld")
        ada_ld = [sem(f"ada_ld{s}") for s in range(4)]
        ada_used, ada_out, ada_turned, c_ready = sem("ada_used"), sem("ada_out"), sem("ada_turned"), sem("c_ready")
        p0_dve, p0_act = sem("p0_dve"), sem("p0_act")
        sq1_done, ss1_done, rt1_done, rs1_done = sem("sq1_done"), sem("ss1_done"), sem("rt1_done"), sem("rs1_done")
        h1_done, h1_hi_done, ba_done, ba_read = sem("h1_done"), sem("h1_hi_done"), sem("ba_done"), sem("ba_read")
        p0_beta, p0_abs, p0_log, g_done, gc_done, gc_read, eg_ready = (
            sem("p0_beta"), sem("p0_abs"), sem("p0_log"), sem("g_done"), sem("gc_done"), sem("gc_read"), sem("eg_ready"))

        def norm_affine(dve, st, h_, x_, rstd, affine, shift, h_done):
            for k in range(KC):
                st(nc.vector.tensor_tensor(h_[:, k, :], x_[:, k, :], rstd[:], ALU.mult))
            st.settle()
            for k in range(KC):
                nc.vector.tensor_scalar(h_[:, k, 0:TP], h_[:, k, 0:TP], affine[:, k, 0:1],
                                        mod[:, shift + k, 0:1], ALU.mult, ALU.add)
            a = affine[:, :, 1:NG].unsqueeze(3).to_broadcast([P, KC, NSEQ, LS])
            b = mod[:, shift:shift + KC, 1:NG].unsqueeze(3).to_broadcast([P, KC, NSEQ, LS])
            st(nc.vector.tensor_tensor(sample_cols(h_), sample_cols(h_), a, ALU.mult))
            st.settle()
            nc.vector.tensor_tensor(sample_cols(h_), sample_cols(h_), b, ALU.add).then_inc(h_done, 1)

        def split_act(dve, src, hi_done, lo_done):
            dve.wait_ge(hi_done, 2)
            for half in range(2):
                ks = slice(half * KC // 2, (half + 1) * KC // 2)
                last = nc.vector.tensor_tensor(act_lo[:, ks, :], src[:, ks, :], act_hi[:, ks, :].bitcast(F32),
                                               ALU.subtract)
            last.then_inc(lo_done, 1)

        def hi_act(act, src, hi_done):
            for half in range(2):
                ks = slice(half * KC // 2, (half + 1) * KC // 2)
                nc.scalar.activation(act_hi[:, ks, :], src[:, ks, :], ACT.Copy).then_inc(hi_done, 1)

        ended, now = [], list(phase_sems)
        phase_sems.clear()
        with nc.Block() as block:
            @block.sync
            def _(sp):
                sp.dma_start(vec[:], vec_in).then_inc(small_ld, 16)
                sp.dma_start(cst[:], cst_in).then_inc(small_ld, 16)
                sp.dma_start(c_raw[:], c_in).then_inc(small_ld, 16)
                sp.dma_start(wba[:], wba_in).then_inc(small_ld, 16)
                sp.dma_start(x[:], x_in).then_inc(x_ld, 16)
                for n in range(N_ADA):
                    if n >= 4:
                        sp.wait_ge(ada_used, n - 3)
                    sp.dma_start(ada_w[n % 4][:], ada_in[n]).then_inc(ada_ld[n % 4], 16)
                for n in range(2):
                    load_chunk(sp, Chunk(n))

            @block.tensor
            def _(pe):
                for s in range(2):
                    pe.sem_inc(pp_done[s], 1)
                    pe.sem_inc(pp_read[s], 1)
                pe.wait_ge(small_ld, 64)
                for k in range(KC):
                    pe.wait_ge(sq1_done, k + 1)
                    for b in range(2):
                        last = nc.tensor.matmul(pp[0][:, b, 0:HN], ones, sq1[:, k, b * HN:(b + 1) * HN],
                                                start=(k == 0), stop=(k == KC - 1))
                last.then_inc(ss1_done, 1)
                pe.wait_ge(c_ready, 1)

                def ada(n):
                    pe.wait_ge(ada_ld[n % 4], 16 * (n // 4) + 16)
                    if n >= 4:
                        pe.wait_ge(ada_out, n - 3)
                    for k in range(KC):
                        last = nc.tensor.matmul(dd[0:NG, n % 4, :], c_silu[:, k, :], ada_w[n % 4][:, k, :],
                                                start=(k == 0), stop=(k == KC - 1))
                    last.then_inc(ada_used, 1)

                def turn(n):
                    pe.wait_ge(ada_out, n + 1)
                    first = n < N_ADA1
                    if n == N_ADA1:
                        pe.wait_ge(rt1_done, 1)
                    for m in range(4):
                        at = (4 * (n if first else n - N_ADA1) + m) * NG
                        last = nc.tensor.transpose((pp[1] if first else pp[0])[:, 0 if first else 1, at:at + NG],
                                                   ada_t[0:NG, n % 4, m * P:(m + 1) * P],
                                                   cst[0:NG, CST["ident"][0]:CST["ident"][0] + NG])
                    last.then_inc(ada_turned, 1)

                for n in range(N_ADA1):
                    ada(n)
                    if n:
                        turn(n - 1)
                turn(N_ADA1 - 1)
                for n in range(N_ADA1, 7):
                    ada(n)
                    if n > N_ADA1:
                        turn(n - 1)
                pe.wait_ge(h1_done, 1)
                for t in range(TT):
                    m = P if t < NC else TS
                    for k in range(KC):
                        last = nc.tensor.matmul(pp[1][0:m, 1, t * 2 * H:(t + 1) * 2 * H], h1[:, k, t * P:t * P + m],
                                                wba[:, k, :], start=(k == 0), stop=(k == KC - 1))
                last.then_inc(ba_done, 1)
                for n in range(7, 9):
                    ada(n)
                    turn(n - 1)
                pe.wait_ge(g_done, 1)
                g_p = tok[:, GRAW, 0:NC, :]
                g_s = tok[0:TS, GRAW, NC, :]
                nc.tensor.matmul(pp[0][:, 0, 0:32], ut, g_p, start=True, stop=True)
                nc.tensor.matmul(pp[0][:, 0, 32:64], ones, g_p, start=True, stop=True)
                nc.tensor.matmul(pp[0][0:TS, 0, 64:72], c_("uts", TS), g_s, start=True, stop=True)
                nc.tensor.matmul(pp[0][0:TS, 0, 72:80], c_("bds", TS), g_s, start=True, stop=True).then_inc(gc_done, 1)
                for n in range(9, N_ADA):
                    ada(n)
                    turn(n - 1)
                turn(N_ADA - 1)

            @block.scalar
            def _(act):
                a_ = Steps(act, p0_act)
                act.wait_ge(small_ld, 64)
                nc.scalar.activation(c_silu[:], c_raw[:], ACT.Silu).then_inc(c_ready, 1)
                act.wait_ge(x_ld, 16)
                for k in range(KC):
                    nc.scalar.activation(sq1[:, k, :], x[:, k, :], ACT.Square).then_inc(sq1_done, 1)
                act.wait_ge(ss1_done, 1)
                act.wait_ge(p0_dve, 2)
                nc.scalar.activation(halves(rstd1[:]), pp[0][:, :, 0:HN], ACT.Sqrt, bias=eps[:],
                                     scale=1.0 / D).then_inc(rt1_done, 1)

                def ada_read(ns):
                    for n in ns:
                        act.wait_ge(ada_used, n + 1)
                        if n >= 4:
                            act.wait_ge(ada_turned, n - 3)
                        nc.scalar.activation(ada_t[0:NG, n % 4, :], dd[0:NG, n % 4, :], ACT.Copy).then_inc(ada_out, 1)

                ada_read(range(6))
                act.wait_ge(h1_done, 1)
                hi_act(act, h1, h1_hi_done)
                ada_read(range(6, 7))
                act.wait_ge(ba_read, 1)
                nc.scalar.activation(tok[:, BETA], ba[:, :, 0:H], ACT.Sigmoid).then_inc(p0_beta, 1)
                act.wait_ge(p0_abs, 1)
                a_(nc.scalar.activation(tmp_b[:], tmp_a[:], ACT.Abs))
                a_.settle()
                a_(nc.scalar.activation(tmp_b[:], tmp_b[:], ACT.Exp, scale=-1.0))
                a_(nc.scalar.activation(ea_log[:], v_("a_log"), ACT.Exp))
                a_.settle()
                nc.scalar.activation(tmp_b[:], tmp_b[:], ACT.Ln, bias=one[:]).then_inc(p0_log, 1)
                ada_read(range(7, 9))
                act.wait_ge(gc_read, 1)
                a_(nc.scalar.activation(tmp_c[:], tok[:, GCUM], ACT.Exp))
                nc.scalar.activation(tok[:, ETAIL], tmp_b[:], ACT.Exp)
                a_(nc.scalar.activation(tok[:, ETOT], tok[:, ETOT], ACT.Exp))
                a_.settle()
                act.sem_inc(eg_ready, 1)
                ada_read(range(9, N_ADA))
                split_hi(act, Chunk(0))

            @block.vector
            def _(dve):
                nc.vector.memset(eps[:], EPS).then_inc(p0_dve, 1)
                nc.vector.memset(one[:], 1.0).then_inc(p0_dve, 1)
                st = Steps(dve, p0_dve, 2)
                st(nc.vector.memset(ba[:, NC, :], 0.0))
                st(nc.vector.memset(tok[:, :, NC, :], 0.0))

                def conditioning(lo, hi, src, aff, sc, g):
                    bias = v_("b_ada")[:, lo:hi].unsqueeze(2).to_broadcast([P, hi - lo, NG])
                    st(nc.vector.tensor_tensor(mod[:, lo:hi, :], src[:, 0:(hi - lo) * NG].rearrange(
                        "p (m g) -> p m g", g=NG), bias, ALU.add))
                    st.settle()
                    st(nc.vector.scalar_tensor_tensor(out=aff[:], in0=mod[:, sc:sc + KC, :], scalar=1.0,
                                                      in1=v_(g).unsqueeze(2).to_broadcast([P, KC, NG]),
                                                      op0=ALU.add, op1=ALU.mult))

                dve.wait_ge(ada_turned, N_ADA1)
                conditioning(0, 4 * N_ADA1, pp[1][:, 0, :], aff1, SC1, "g1")
                dve.wait_ge(rt1_done, 1)
                st(nc.vector.reciprocal(rstd1[:], rstd1[:]))
                st.settle()
                norm_affine(dve, st, h1, x, rstd1, aff1, SH1, h1_done)
                split_act(dve, h1, h1_hi_done, rs1_done)
                dve.wait_ge(ba_done, 1)
                st(nc.vector.tensor_copy(ba[:, 0:NC, :], pp[1][:, 1, 0:NC * 2 * H].rearrange("p (t n) -> p t n", t=NC)))
                st(nc.vector.tensor_copy(ba[0:TS, NC, :], pp[1][0:TS, 1, NC * 2 * H:TT * 2 * H]))
                st.settle()
                dve.sem_inc(ba_read, 1)
                nc.vector.tensor_tensor(tmp_a[:], ba[:, :, H:2 * H], v_("dt").unsqueeze(1).to_broadcast([P, TT, H]),
                                        ALU.add).then_inc(p0_abs, 1)
                dve.wait_ge(p0_log, 1)
                st(nc.vector.scalar_tensor_tensor(out=tmp_a[:], in0=tmp_a[:], scalar=0.0, in1=tmp_b[:],
                                                  op0=ALU.max, op1=ALU.add))
                st.settle()
                nc.vector.scalar_tensor_tensor(out=tok[:, GRAW], in0=tmp_a[:], scalar=-1.0,
                                               in1=ea_log[:].unsqueeze(1).to_broadcast([P, TT, H]),
                                               op0=ALU.mult, op1=ALU.mult).then_inc(g_done, 1)
                dve.wait_ge(gc_done, 1)
                for n, what in enumerate((GCUM, ETOT)):
                    st(nc.vector.tensor_copy(tok[:, what, 0:NC, :],
                                             pp[0][:, 0, 32 * n:32 * n + 32].rearrange("p (t h) -> p t h", t=NC)))
                    st(nc.vector.tensor_copy(tok[0:TS, what, NC, :], pp[0][0:TS, 0, 64 + 8 * n:72 + 8 * n]))
                st.settle()
                nc.vector.tensor_tensor(tmp_b[:], tok[:, ETOT], tok[:, GCUM], ALU.subtract).then_inc(gc_read, 1)
                dve.wait_ge(eg_ready, 1)
                st(nc.vector.scalar_tensor_tensor(out=tok[:, NBEG], in0=tmp_c[:], scalar=-1.0, in1=tok[:, BETA],
                                                  op0=ALU.mult, op1=ALU.mult))
                dve.wait_ge(ada_turned, N_ADA)
                conditioning(4 * N_ADA1, 6 * KC, pp[0][:, 1, :], aff2, SC2, "g2")
                split_lo(dve, Chunk(0))
                st.settle()

        pool_ld, pool_z = sem("pool_ld"), sem("pool_z")
        zg_done, pool_copied, p1_dve, pooled_done = sem("zg_done"), sem("pool_copied"), sem("p1_dve"), sem("pooled_done")
        py_done, py_read = sem("py_done"), sem("py_read")

        ended, now = now, list(phase_sems)
        phase_sems.clear()
        with nc.Block() as block:
            @block.gpsimd
            def _(pool):
                retire(pool, ended)

            @block.sync
            def _(sp):
                sp.dma_start(pool_st[:], pool_in).then_inc(pool_ld, 16)
                sp.dma_start(wpool[:], wpool_in).then_inc(pool_ld, 16)
                sp.dma_start(conv_st[:], conv_in).then_inc(pool_ld, 16)
                with sp.Fori(0, C_QKV // 2) as i:
                    for o in range(2):
                        load_chunk(sp, Chunk(2, o, 2, i))
                sp.wait_ge(pool_ld, 48)

            @block.tensor
            def _(pe):
                with pe.Fori(0, C_QKV // 2) as i:
                    for o in range(2):
                        product(pe, Chunk(0, o, 2, i))
                pe.wait_ge(pool_ld, 48)
                for m in range(KC):
                    g = m // 2
                    if m % 2 == 0:
                        pe.wait_ge(pooled_done, g + 1)
                    if m >= 2:
                        pe.wait_ge(py_read, m - 1)
                    for b in range(2):
                        last = nc.tensor.matmul(dd[:, 2 * (m % 2) + b, 0:HN], wpool[:, g, (m % 2) * P:(m % 2 + 1) * P],
                                                pooled[:, g, b * HN:(b + 1) * HN], start=True, stop=True)
                    last.then_inc(py_done, 1)

            @block.scalar
            def _(act):
                def each(base, n, into, func):
                    with act.Fori(0, n // 2) as i:
                        for o in range(2):
                            k = Chunk(base, o, 2, i)
                            split_hi(act, k + 1)
                            gate_act(act, pp_done[k.slot], k.turn + 2)
                            out, wait = into(i, o, k)
                            if wait:
                                gate_act(act, *wait)
                            nc.scalar.activation(out, pp[k.slot][:, :, 0:HN], func).then_inc(pp_read[k.slot], 1)

                def col(t, i, o):
                    return t[:, bass.ds(2 * i + o, 1), :].rearrange("p a (b n) -> p (a b) n", b=2)

                each(C_Z, N_Z, lambda i, o, k: (col(zg, i, o), None), ACT.Silu)
                each(C_GA, N_GA, lambda i, o, k: (halves(sig[k.slot][:]), (zg_done, 2 * i + o + 1)), ACT.Sigmoid)
                for g in range(N_POOL):
                    k = Chunk(C_POOL + g)
                    split_hi(act, k + 1)
                    done(act, k)
                    nc.scalar.activation(pbuf[:, g, PB_:PB_ + HN], pp[k.slot][:, 0, 0:HN], ACT.Copy)
                    nc.scalar.activation(pbuf[:, g, PB_ + HN:PS0], pp[k.slot][:, 1, 0:TP - HN], ACT.Copy)
                    seg = pbuf[:, g, PS0:PBW].rearrange("p (s t) -> p s t", s=NSEQ)[:, :, PB_:SEG_P]
                    nc.scalar.activation(seg, pp[k.slot][:, 1, TP - HN:HN].rearrange("p (s t) -> p s t", s=NSEQ),
                                         ACT.Copy).then_inc(pp_read[k.slot], 1)
                each(C_GB, N_GB, lambda i, o, k: (col(mixed, i, o), None), ACT.Sigmoid)

            @block.vector
            def _(dve):
                st = Steps(dve, p1_dve)
                dve.sem_inc(zg_done, 2)
                dve.wait_ge(pool_ld, 48)
                for g in range(len(WINDOWS)):
                    st(nc.vector.memset(pbuf[:, g, 0:PB_], 0.0))
                    st(nc.vector.tensor_copy(pbuf[:, g, PS0:PBW].rearrange("p (s t) -> p s t", s=NSEQ)[:, :, 0:PB_],
                                             pool_st[:, g]))
                with dve.Fori(0, N_Z // 2) as i:
                    for o in range(2):
                        split_lo(dve, Chunk(C_Z, o, 2, i) + 1)
                with dve.Fori(0, N_GA // 2) as i:
                    for o in range(2):
                        k = Chunk(C_GA, o, 2, i)
                        split_lo(dve, k + 1)
                        read(dve, k)
                        z = zg[:, bass.ds(2 * i + o, 1), :].rearrange("p a n -> p (a n)")
                        nc.vector.tensor_tensor(z, z, sig[k.slot][:], ALU.mult).then_inc(zg_done, 1)
                for g, w in enumerate(WINDOWS):
                    k = Chunk(C_POOL + g)
                    split_lo(dve, k + 1)
                    read(dve, k)
                    st.settle()
                    src, lo = pbuf[:, g, :], 0
                    for n in range(g + 1):
                        dst = psum_w[n % 2][:]
                        lo += 1 << n
                        st(nc.vector.tensor_tensor(dst[:, lo:PBW], src[:, lo:PBW], src[:, lo - (1 << n):PBW - (1 << n)],
                                                   ALU.add))
                        st.settle()
                        src = dst
                    spare = psum_w[(g + 1) % 2][:, 0:16]
                    st(nc.vector.scalar_tensor_tensor(out=pooled[:, g, 0:TP], in0=src[:, PB_:PS0], scalar=1.0 / w,
                                                      in1=pbuf[:, g, PB_:PS0], op0=ALU.mult, op1=ALU.subtract))
                    rc = cst[:, CST["rc"][0] + 16 * g:CST["rc"][0] + 16 * g + 16]
                    st(nc.vector.tensor_tensor(spare, src[:, PB_:PB_ + 16], rc, ALU.mult))

                    def seg(t):
                        return t[:, PS0:PBW].rearrange("p (s t) -> p s t", s=NSEQ)[:, :, PB_:SEG_P]

                    st(nc.vector.scalar_tensor_tensor(
                        out=pooled[:, g, TP:NT].rearrange("p (s t) -> p s t", s=NSEQ), in0=seg(src), scalar=1.0 / w,
                        in1=seg(pbuf[:, g, :]), op0=ALU.mult, op1=ALU.subtract))
                    st(nc.vector.tensor_copy(pool_new[:, g, 0, :], pbuf[:, g, PS0 - PB_:PS0]))
                    st(nc.vector.tensor_copy(pool_new[:, g, 1:NG, :],
                                             pbuf[:, g, PS0:PBW].rearrange("p (s t) -> p s t", s=NSEQ)[:, :, LS:SEG_P]))
                    st.settle()
                    nc.vector.tensor_tensor(pooled[:, g, 0:16], spare, pbuf[:, g, PB_:PB_ + 16],
                                            ALU.subtract).then_inc(pooled_done, 1)
                    dve.wait_ge(pooled_done, g + 1)
                with dve.Fori(0, N_GB // 2) as i:
                    for o in range(2):
                        split_lo(dve, Chunk(C_GB, o, 2, i) + 1)
                for s in range(2):
                    read(dve, Chunk(C_QKV - 2 + s))
                for m in range(KC):
                    dve.wait_ge(py_done, m + 1)
                    o = halves(mixed[:, m, :])
                    nc.vector.scalar_tensor_tensor(out=o, in0=dd[:, 2 * (m % 2):2 * (m % 2) + 2, 0:HN],
                                                   scalar=vec[:, VEC["pool_scale"][0] + m:VEC["pool_scale"][0] + m + 1],
                                                   in1=o, op0=ALU.mult, op1=ALU.mult).then_inc(py_read, 1)
                dve.wait_ge(py_read, KC)

        out_st = sem("out_st")
        n_out = [0]
        s_ld = sem("s_ld")
        conv_done = sem("conv_done")
        head_done = sem("head_done")
        silu_done, sq_done, ss_done, rs_done, qk_ready = (
            sem("silu_done"), sem("sq_done"), sem("ss_done"), sem("rs_done"), sem("qk_ready"))
        hs_ready, grow_done, brow_done, egrow_done, dmin_done, dexp_done, kb_ready, qe_ready = (
            sem("hs_ready"), sem("grow_done"), sem("brow_done"), sem("egrow_done"), sem("dmin_done"),
            sem("dexp_done"), sem("kb_ready"), sem("qe_ready"))
        kk_done, ktr_done, vtr_done, kt_ready, vb_ready, qkm_ready = (
            sem("kk_done"), sem("ktr_done"), sem("vtr_done"), sem("kt_ready"), sem("vb_ready"), sem("qkm_ready"))
        lm_ready, tu_ready, tr_done, ti_ready, a_done, ap_ready, dti_done, dtu_done, ap_zero = (
            sem("lm_ready"), sem("tu_ready"), sem("tr_done"), sem("ti_ready"), sem("a_done"), sem("ap_ready"),
            sem("dti_done"), sem("dtu_done"), sem("ap_zero"))
        ks_done, r_ready, vn_done, vn_ready, o_done, ds_done, s_ready = (
            sem("ks_done"), sem("r_ready"), sem("vn_done"), sem("vn_ready"), sem("o_done"), sem("ds_done"),
            sem("s_ready"))
        osq_done, oss_done, ors_done, o_read = sem("osq_done"), sem("oss_done"), sem("ors_done"), sem("o_read")
        p2_dve, p2_act = sem("p2_dve"), sem("p2_act")

        def tiles(t):
            return t.rearrange("p (c n) -> p c n", c=NC)

        def b_cols(a):
            return a.unsqueeze(2).to_broadcast([P, NC, P])

        def b_tile(a):
            return a.unsqueeze(1).to_broadcast([P, NC, P])

        def part(t, n, half):
            return t.rearrange("p (b two s) -> p b two s", two=2, s=2 << n)[:, :, half, :]

        def packed(t, n):
            return t.rearrange("p (b s) -> p b s", s=2 << n)

        def heads_in_turn(eng, first, turn):
            def chunks(i, head):
                return [Chunk(C_QKV, 3 * head + r, 6, i) for r in range(3)]

            first([Chunk(C_QKV, r) for r in range(3)])
            with eng.Fori(0, H // 2 - 1) as i:
                turn(2 * i, 0, chunks(i, 1))
                turn(2 * i + 1, 1, chunks(i, 2))
            turn(H - 2, 0, chunks(H // 2 - 1, 1))
            turn(H - 1, 1, None)

        PIECES = {"norm": 6, "beta": 4, "inverse": 6, **{f"level {n}": 1 for n in range(NLV)}, "scan 0": 2}
        assert sum(PIECES.values()) == 3 * KC

        ended, now = now, list(phase_sems)
        phase_sems.clear()
        with nc.Block() as block:
            @block.gpsimd
            def _(pool):
                retire(pool, ended)
                for n in range(NLV):
                    nc.gpsimd.memset(ap_[n][:], 0.0).then_inc(ap_zero, 1)

            @block.sync
            def _(sp):
                with sp.Fori(0, 12) as i:
                    for o in range(2):
                        load_chunk(sp, Chunk(C_QKV + 2, o, 2, i))
                sp.wait_ge(head_done, H)
                sp.dma_start(delta_p_out, s_fin[:]).then_inc(out_st, 16)
                sp.dma_start(conv_out, conv_new[:]).then_inc(out_st, 16)
                sp.dma_start(pool_out, pool_new[:]).then_inc(out_st, 16)
                n_out[0] += 3

            @block.tensor
            def _(pe):
                def first(chunks):
                    for k in chunks:
                        product(pe, k)

                def head(hv, par, chunks):
                    qkv = qkv_h[par]
                    count = [0]

                    def beside(place):
                        if chunks is not None:
                            for _ in range(PIECES.get(place, 0)):
                                at = count[0]
                                product(pe, chunks[at // KC], range(at % KC, at % KC + 1))
                                count[0] += 1

                    pe.wait_ge(sq_done, hv + 1)
                    for r in range(2):
                        for b in range(2):
                            last = nc.tensor.matmul(dd[:, 2 * r + b, 0:CY // 2], ones,
                                                    qk_sq[:, r, b * (CY // 2):(b + 1) * (CY // 2)],
                                                    start=True, stop=True)
                    last.then_inc(ss_done, 1)
                    beside("norm")
                    pe.wait_ge(hs_ready, hv + 1)
                    pe.wait_ge(rs_done, hv + 1)
                    for c in range(NC):
                        last = nc.tensor.matmul(dd[:, 0, c * P:(c + 1) * P], hs[:, GRAW, c:c + 1].to_broadcast([P, P]),
                                                ut, start=True, stop=True)
                    last.then_inc(grow_done, 1)
                    for c in range(NC):
                        last = nc.tensor.matmul(dd[:, 1, c * P:(c + 1) * P], hs[:, BETA, c:c + 1].to_broadcast([P, P]),
                                                ident, start=True, stop=True)
                    last.then_inc(brow_done, 1)
                    pe.wait_ge(qk_ready, 2 * hv + 2)
                    for c in range(NC):
                        t = slice(c * P, (c + 1) * P)
                        nc.tensor.matmul(dd[:, 3, t], qkv[:, 1, t], qkv[:, 0, t], start=True, stop=True)
                    beside("beta")
                    pe.wait_ge(kb_ready, hv + 1)
                    for c in range(NC):
                        t = slice(c * P, (c + 1) * P)
                        last = nc.tensor.matmul(dd[:, 2, t], qkv[:, 1, t], kb[:, t], start=True, stop=True)
                    last.then_inc(kk_done, 1)
                    pe.wait_ge(silu_done, 3 * hv + 3)
                    for c in range(NC):
                        t = slice(c * P, (c + 1) * P)
                        last = nc.tensor.transpose(dd[:, 1, t], qkv[:, 2, t], ident)
                    last.then_inc(vtr_done, 1)
                    pe.wait_ge(dmin_done, hv + 1)
                    pe.wait_ge(egrow_done, hv + 1)
                    for c in range(NC):
                        t = slice(c * P, (c + 1) * P)
                        last = nc.tensor.transpose(dd[:, 0, t], qkv[:, 1, t], ident)
                    last.then_inc(ktr_done, 1)
                    beside("inverse")
                    pe.wait_ge(tu_ready, (NLV + 1) * hv + 1)
                    for c in range(NC):
                        t = slice(c * P, (c + 1) * P)
                        last = nc.tensor.transpose(dd[:, 2, t], tu[:, t], ident)
                    last.then_inc(tr_done, 1)
                    for n in range(NLV):
                        pe.wait_ge(lm_ready, NLV * hv + n + 1)
                        pe.wait_ge(ti_ready, NLV * hv + n + 1)
                        if n == 0:
                            pe.wait_ge(vb_ready, hv + 1)
                            pe.wait_ge(qkm_ready, hv + 1)
                        for c in range(NC):
                            t = slice(c * P, (c + 1) * P)
                            o = slice(c * P // 2, (c + 1) * P // 2)
                            last = nc.tensor.matmul(packed(dd[:, 1, o], n), lm[n % 2][:, t], part(ti[:, t], n, 0),
                                                    start=True, stop=True)
                        last.then_inc(a_done, 1)
                        beside(f"level {n}")
                        pe.wait_ge(tu_ready, (NLV + 1) * hv + n + 1)
                        pe.wait_ge(ap_ready, NLV * hv + n + 1)
                        if n < NLV - 1:
                            for c in range(NC):
                                t = slice(c * P, (c + 1) * P)
                                o = slice(c * P // 2, (c + 1) * P // 2)
                                last = nc.tensor.matmul(packed(dd[:, 2, o], n), tu[:, t], part(ap_[n][:, t], n, 0),
                                                        start=True, stop=True)
                            last.then_inc(dti_done, 1)
                        for c in range(NC):
                            t = slice(c * P, (c + 1) * P)
                            o = slice(c * P // 2, (c + 1) * P // 2)
                            last = nc.tensor.matmul(packed(dd[:, 3, o], n), ap_[n][:, t], part(tu[:, t], n, 1),
                                                    start=True, stop=True)
                        last.then_inc(dtu_done, 1)
                    pe.wait_ge(tu_ready, (NLV + 1) * hv + NLV + 1)
                    pe.wait_ge(kt_ready, hv + 1)
                    for c in range(NC):
                        t = slice(c * P, (c + 1) * P)
                        if c:
                            pe.wait_ge(s_ready, NC * hv + c)
                            nc.tensor.matmul(dd[:, 0, t], qkv[:, 1, t], s_run[:, (c - 1) % 2, :], start=True,
                                             stop=True).then_inc(ks_done, 1)
                            if c == 1:
                                pe.wait_ge(qe_ready, hv + 1)
                            nc.tensor.matmul(dd[:, 3, t], s_run[:, (c - 1) % 2, :], qe[:, t], start=True, stop=False)
                            pe.wait_ge(r_ready, (NC - 1) * hv + c)
                        nc.tensor.matmul(dd[:, 1, t], tu[:, t], (r_new if c else v_beta)[:, t], start=True,
                                         stop=True).then_inc(vn_done, 1)
                        beside(f"scan {c}")
                        pe.wait_ge(vn_ready, NC * hv + c + 1)
                        nc.tensor.matmul(dd[:, 2, t], k_tail[:, t], v_new[:, t], start=True, stop=True).then_inc(ds_done, 1)
                        nc.tensor.matmul(dd[:, 3, t], v_new[:, t], qk[:, t], start=(c == 0), stop=True).then_inc(o_done, 1)
                    pe.wait_ge(osq_done, hv + 1)
                    nc.tensor.matmul(dd[:, 0, :], ones, o_sq[:], start=True, stop=True).then_inc(oss_done, 1)
                    pe.wait_ge(o_read, hv + 1)

                heads_in_turn(pe, first, head)

            @block.scalar
            def _(act):
                def evac(k, col):
                    done(act, k)
                    act.wait_ge(conv_done, col + 1)
                    b = cbuf[k.slot]
                    nc.scalar.activation(b[:, CW - 1:CW - 1 + HN], pp[k.slot][:, 0, 0:HN], ACT.Copy)
                    nc.scalar.activation(b[:, CW - 1 + HN:CS0], pp[k.slot][:, 1, 0:TP - HN], ACT.Copy)
                    seg = b[:, CS0:CB].rearrange("p (s t) -> p s t", s=NSEQ)[:, :, CW - 1:SEG_C]
                    nc.scalar.activation(seg, pp[k.slot][:, 1, TP - HN:HN].rearrange("p (s t) -> p s t", s=NSEQ),
                                         ACT.Copy).then_inc(pp_read[k.slot], 1)

                def silu(a, par, r):
                    act.wait_ge(conv_done, 3 * a + (r + 3))
                    nc.scalar.activation(qkv_h[par][:, r, 0:CY], qkv_h[par][:, r, 0:CY], ACT.Silu).then_inc(silu_done, 1)

                def squares(a, par):
                    act.wait_ge(silu_done, 3 * a + 2)
                    nc.scalar.activation(qk_sq[:], qkv_h[par][:, 0:2, 0:CY], ACT.Square).then_inc(sq_done, 1)

                def log_exp():
                    act.add_instruction(mybir.InstLoadActFuncSet(
                        name=nc.get_next_instruction_name(), act_func_set_id=LOG_EXP_SET,
                        engine=mybir.EngineType.Activation))

                def first(chunks):
                    for r, k in enumerate(chunks):
                        split_hi(act, k + 1)
                        evac(k, r)
                        if r:
                            silu(0, 0, r - 1)
                    silu(0, 0, 2)
                    squares(0, 0)
                    log_exp()

                def head(hv, par, chunks):
                    qkv = qkv_h[par]
                    nxt = hv + 1
                    n_own = 3
                    a_ = Steps(act, p2_act, n_own * hv)

                    def beside(place):
                        if chunks is None:
                            return
                        if place == "norm":
                            split_hi(act, chunks[0] + 1)
                        elif place == "decay":
                            evac(chunks[0], 3 * nxt)
                            split_hi(act, chunks[1] + 1)
                        elif place == "level 0":
                            evac(chunks[1], 3 * nxt + 1)
                            split_hi(act, chunks[2] + 1)
                        elif place == "level 3":
                            silu(nxt, 1 - par, 0)
                        elif place == "scan 0":
                            silu(nxt, 1 - par, 1)
                            squares(nxt, 1 - par)
                        elif place == "scan 1":
                            evac(chunks[2], 3 * nxt + 2)
                        elif place == "scan 3":
                            silu(nxt, 1 - par, 2)

                    act.wait_ge(ss_done, hv + 1)
                    rs = qk_rs[:].rearrange("p r (b n) -> p (r b) n", b=2)
                    a_(nc.scalar.activation(rs, dd[:, :, 0:CY // 2], ACT.Ln, bias=eps[:]))
                    a_.settle()
                    nc.scalar.activation(rs, rs, ACT.Exp, scale=-0.5).then_inc(rs_done, 1)
                    beside("norm")
                    act.wait_ge(dmin_done, hv + 1)
                    nc.scalar.activation(eg_row[:], dd[:, 0, :], ACT.Exp).then_inc(egrow_done, 1)
                    nc.scalar.activation(decay[:], decay[:], ACT.Exp).then_inc(dexp_done, 1)
                    beside("decay")
                    act.wait_ge(tr_done, hv + 1)
                    nc.scalar.activation(ti[:], dd[:, 2, :], ACT.Copy).then_inc(ti_ready, 1)
                    for n in range(NLV):
                        act.wait_ge(a_done, NLV * hv + n + 1)
                        nc.scalar.activation(part(ap_[n][:], n, 0), packed(dd[:, 1, 0:TP // 2], n),
                                             ACT.Copy).then_inc(ap_ready, 1)
                        beside(f"level {n}")
                    for c in range(NC):
                        t = slice(c * P, (c + 1) * P)
                        act.wait_ge(vn_done, NC * hv + c + 1)
                        nc.scalar.activation(v_new[:, t], dd[:, 1, t], ACT.Copy).then_inc(vn_ready, 1)
                        beside(f"scan {c}")
                    if chunks is not None:
                        log_exp()
                    act.wait_ge(o_done, NC * hv + NC)
                    nc.scalar.activation(o_sq[:], dd[:, 3, :], ACT.Square).then_inc(osq_done, 1)
                    act.wait_ge(oss_done, hv + 1)
                    a_(nc.scalar.activation(o_rs[:], dd[:, 0, :], ACT.Ln, bias=eps[:], scale=1.0 / P))
                    a_.settle()
                    a_(nc.scalar.activation(o_rs[:], o_rs[:], ACT.Exp, scale=-0.5))
                    a_.settle()
                    act.sem_inc(ors_done, 1)
                    assert a_.n == n_own

                act.wait_ge(ap_zero, NLV)
                heads_in_turn(act, first, head)

            @block.vector
            def _(dve):
                n_conv = 6
                n_head = 7
                for s in range(2):
                    nc.vector.memset(cbuf[s][:, 0:CW - 1], 0.0).then_inc(p2_dve, 1)
                dve.wait_ge(p2_dve, 2)
                dve.sem_inc(conv_done, 2)

                def conv(st, k, a, par, r, taps):
                    col = 3 * a + r
                    b = cbuf[k.slot]

                    def w(tap):
                        return vec[:, bass.ds(col * CW + (VEC["conv_w"][0] + tap), 1)]

                    y = qkv_h[par][:, r, 0:CY]
                    for tap in taps:
                        if tap == 0:
                            segs = b[:, CS0:CB].rearrange("p (s t) -> p s t", s=NSEQ)
                            old = conv_st[:, bass.ds(col, 1), :, :].rearrange("p a s t -> p (a s) t")
                            new = conv_new[:, bass.ds(col, 1), :, :].rearrange("p a s t -> p (a s) t")
                            gate_dve(dve, pp_read[k.slot], k.turn + 2)
                            st(nc.vector.tensor_copy(segs[:, :, 0:CW - 1], old))
                            st(nc.vector.tensor_copy(new[:, 0:1, :], b[:, CS0 - CW + 1:CS0].unsqueeze(1)))
                            st(nc.vector.tensor_copy(new[:, 1:NG, :], segs[:, :, LS:SEG_C]))
                            st.settle()
                            st(nc.vector.tensor_scalar(y, b[:, 0:CY], w(0), None, ALU.mult))
                            continue
                        st.settle()
                        ins = nc.vector.scalar_tensor_tensor(out=y, in0=b[:, tap:tap + CY], scalar=w(tap), in1=y,
                                                             op0=ALU.mult, op1=ALU.add)
                        if tap < CW - 1:
                            st(ins)
                        else:
                            ins.then_inc(conv_done, 1)

                def first(chunks):
                    st = Steps(dve, p2_dve, 2)
                    for r, k in enumerate(chunks):
                        split_lo(dve, k + 1)
                        conv(st, k, 0, 0, r, range(CW))
                    assert st.n == 3 * n_conv

                def head(hv, par, chunks):
                    qkv = qkv_h[par]
                    st = Steps(dve, p2_dve, (3 * n_conv + n_head) * hv + (2 + 3 * n_conv))

                    def beside(place):
                        if chunks is None:
                            return
                        if place == "norm":
                            split_lo(dve, chunks[0] + 1)
                        elif place == "inverse":
                            split_lo(dve, chunks[1] + 1)
                        elif place == "scan 0":
                            split_lo(dve, chunks[2] + 1)
                        r, taps = {"level 0": (0, (0, 1)), "level 1": (0, (2, 3)), "level 2": (1, (0,)),
                                   "level 3": (1, (1,)), "level 4": (1, (2,)), "level 5": (1, (3,)),
                                   "scan 1": (2, (0,)), "scan 2": (2, (1, 2)), "scan 3": (2, (3,))}.get(place, (0, ()))
                        conv(st, chunks[r], hv + 1, 1 - par, r, taps)

                    gate_dve(dve, silu_done, 3 * hv + 3)
                    nc.vector.tensor_copy(hs[:].unsqueeze(3), tok[:, :, :, bass.ds(hv, 1)]).then_inc(hs_ready, 1)
                    beside("norm")
                    dve.wait_ge(hs_ready, hv + 1)
                    dve.wait_ge(rs_done, hv + 1)
                    nc.vector.scalar_tensor_tensor(out=qkv[:, 0, 0:CY], in0=qkv[:, 0, 0:CY], scalar=float(P) ** -0.5,
                                                   in1=qk_rs[:, 0, :], op0=ALU.mult, op1=ALU.mult).then_inc(qk_ready, 1)
                    nc.vector.tensor_tensor(qkv[:, 1, 0:CY], qkv[:, 1, 0:CY], qk_rs[:, 1, :],
                                            ALU.mult).then_inc(qk_ready, 1)
                    dve.wait_ge(grow_done, hv + 1)
                    for c in range(NC):
                        t = slice(c * P, (c + 1) * P)
                        last = nc.vector.tensor_scalar(decay[:, t], dd[:, 0, t], hs[:, GCUM, c:c + 1], 0.0,
                                                       ALU.subtract, ALU.min)
                    last.then_inc(dmin_done, 1)
                    dve.wait_ge(brow_done, hv + 1)
                    dve.wait_ge(qk_ready, 2 * hv + 2)
                    nc.vector.tensor_tensor(kb[:], qkv[:, 1, 0:TP], dd[:, 1, :], ALU.mult).then_inc(kb_ready, 1)
                    dve.wait_ge(dexp_done, hv + 1)
                    st(nc.vector.tensor_tensor(tiles(decay[:]), tiles(decay[:]), b_tile(ut), ALU.mult))
                    st.settle()
                    dve.wait_ge(kk_done, hv + 1)
                    st(nc.vector.tensor_tensor(lt[:], dd[:, 2, :], decay[:], ALU.mult))
                    st.settle()
                    st(nc.vector.tensor_tensor(tiles(tu[:]), tiles(lt[:]), b_tile(level(0)), ALU.mult))
                    st.settle()
                    nc.vector.tensor_tensor(tiles(tu[:]), b_tile(ident), tiles(tu[:]), ALU.subtract).then_inc(tu_ready, 1)
                    nc.vector.tensor_tensor(tiles(lm[0][:]), tiles(lt[:]), b_tile(level(1)), ALU.mult).then_inc(lm_ready, 1)
                    nc.vector.tensor_tensor(qk[:], dd[:, 3, :], decay[:], ALU.mult).then_inc(qkm_ready, 1)
                    dve.wait_ge(vtr_done, hv + 1)
                    nc.vector.tensor_tensor(tiles(v_beta[:]), tiles(dd[:, 1, :]), b_cols(hs[:, BETA, 0:NC]),
                                            ALU.mult).then_inc(vb_ready, 1)
                    beside("inverse")
                    for n in range(NLV):
                        if n < NLV - 1:
                            nc.vector.tensor_tensor(tiles(lm[(n + 1) % 2][:]), tiles(lt[:]), b_tile(level(n + 2)),
                                                    ALU.mult).then_inc(lm_ready, 1)
                            dve.wait_ge(ti_ready, NLV * hv + n + 1)
                            dve.wait_ge(dti_done, (NLV - 1) * hv + n + 1)
                            nc.vector.tensor_tensor(part(ti[:], n, 0), part(ti[:], n, 0), packed(dd[:, 2, 0:TP // 2], n),
                                                    ALU.subtract).then_inc(ti_ready, 1)
                        dve.wait_ge(tu_ready, (NLV + 1) * hv + n + 1)
                        dve.wait_ge(dtu_done, NLV * hv + n + 1)
                        nc.vector.tensor_tensor(part(tu[:], n, 1), part(tu[:], n, 1), packed(dd[:, 3, 0:TP // 2], n),
                                                ALU.subtract).then_inc(tu_ready, 1)
                        if n == 0:
                            dve.wait_ge(ktr_done, hv + 1)
                            nc.vector.tensor_tensor(tiles(k_tail[:]), tiles(dd[:, 0, :]), b_cols(hs[:, ETAIL, 0:NC]),
                                                    ALU.mult).then_inc(kt_ready, 1)
                        elif n == 1:
                            dve.wait_ge(egrow_done, hv + 1)
                            nc.vector.tensor_tensor(qe[:], qkv[:, 0, 0:TP], eg_row[:], ALU.mult).then_inc(qe_ready, 1)
                        beside(f"level {n}")
                    seg = qkv[:, :, CS0:CB].rearrange("p r (s t) -> p r s t", s=NSEQ)[:, :, :, 0:LS]
                    for c in range(NC):
                        t = slice(c * P, (c + 1) * P)
                        if c:
                            dve.wait_ge(ks_done, (NC - 1) * hv + c)
                            dve.wait_ge(vb_ready, hv + 1)
                            nc.vector.scalar_tensor_tensor(out=r_new[:, t], in0=dd[:, 0, t], scalar=hs[:, NBEG, c:c + 1],
                                                           in1=v_beta[:, t], op0=ALU.mult, op1=ALU.add).then_inc(r_ready, 1)
                            out = qkv_s[:, bass.ds(hv, 1), c - 1, :].rearrange("p a (s t) -> p (a s) t", s=NSEQ)
                            st(nc.vector.tensor_copy(out, seg[:, c - 1]))
                        gate_dve(dve, ds_done, NC * hv + c + 1)
                        dst = s_run[:, c % 2, :]
                        if c == 0:
                            nc.vector.tensor_copy(dst, dd[:, 2, t]).then_inc(s_ready, 1)
                        else:
                            if c == NC - 1:
                                dst = s_fin[:, bass.ds(hv, 1), :].rearrange("p a n -> p (a n)")
                            gate_dve(dve, s_ready, NC * hv + c)
                            nc.vector.scalar_tensor_tensor(out=dst, in0=s_run[:, (c - 1) % 2, :],
                                                           scalar=hs[:, ETOT, c:c + 1], in1=dd[:, 2, t],
                                                           op0=ALU.mult, op1=ALU.add).then_inc(s_ready, 1)
                        beside(f"scan {c}")
                    dve.wait_ge(ors_done, hv + 1)
                    nc.vector.tensor_tensor(o_t[:], dd[:, 3, :], o_rs[:], ALU.mult).then_inc(o_read, 1)
                    dve.wait_ge(o_read, hv + 1)
                    z = zg[:, bass.ds(hv, 1), 0:TP].rearrange("p a n -> p (a n)")
                    m = mixed[:, bass.ds(hv, 1), 0:TP].rearrange("p a n -> p (a n)")
                    st(nc.vector.scalar_tensor_tensor(out=o_t[:], in0=o_t[:], scalar=v_("dn_g"), in1=z,
                                                      op0=ALU.mult, op1=ALU.mult))
                    st.settle()
                    nc.vector.tensor_tensor(m, m, o_t[:], ALU.add).then_inc(head_done, 1)
                    assert chunks is None or st.n == 3 * n_conv + n_head, st.n

                heads_in_turn(dve, first, head)
                dve.wait_ge(head_done, H)

        s3 = {n: sem("s3_" + n) for n in (
            "grow", "brow", "egrow", "dsub", "dexp", "kb", "qe", "qk", "kk", "ktr", "vtr", "qkm", "tu", "tr", "ti",
            "lm", "a", "ap", "du", "kt", "vb", "ks", "ksc", "kst", "r", "vn", "vnc", "o", "osq", "oss", "ors", "km",
            "ds", "snew", "dve", "act", "mix", "kst_read")}
        GH = 4

        def head_cols(a, rows=TS, n=TS):
            return a.unsqueeze(2).to_broadcast([rows, H, n])

        def head_tile(a):
            return a.unsqueeze(1).to_broadcast([TS, H, TS])

        ended, now = now, list(phase_sems)
        phase_sems.clear()
        with nc.Block() as block:
            @block.gpsimd
            def _(pool):
                retire(pool, ended)

            @block.sync
            def _(sp):
                for h in range(H):
                    sp.dma_start(s_s[:, h], delta_in[h]).then_inc(s_ld, 16)
                for h in range(H):
                    sp.wait_ge(s3["snew"], 2 * h + 2)
                    sp.dma_start(delta_s_out[h], s_s[:, h]).then_inc(out_st, 16)
                    n_out[0] += 1
                sp.wait_ge(out_st, 16 * n_out[0])

            def q_(h):
                return qkv_s[:, h, 0, :]

            def k_(h):
                return qkv_s[:, h, 1, :]

            @block.tensor
            def _(pe):
                def cols(bank, h, rows=P):
                    return dd[0:rows, bank, h * TS:(h + 1) * TS]

                for h in range(H):
                    last = nc.tensor.matmul(cols(0, h), tok[0:TS, GRAW, NC, h:h + 1].to_broadcast([TS, P]),
                                            c_("uts", TS), start=True, stop=True)
                last.then_inc(s3["grow"], 1)
                for h in range(H):
                    last = nc.tensor.matmul(cols(1, h), tok[0:TS, BETA, NC, h:h + 1].to_broadcast([TS, P]),
                                            cst[0:TS, CST["ident"][0]:CST["ident"][0] + TS], start=True, stop=True)
                last.then_inc(s3["brow"], 1)
                for h in range(H):
                    last = nc.tensor.matmul(cols(3, h, TS), k_(h), q_(h), start=True, stop=True)
                last.then_inc(s3["qk"], 1)
                pe.wait_ge(s3["kb"], 1)
                for h in range(H):
                    last = nc.tensor.matmul(cols(2, h, TS), k_(h), kb_s[:, h, :], start=True, stop=True)
                last.then_inc(s3["kk"], 1)

                def token_major(src, tile_, s):
                    for h in range(H):
                        last = nc.tensor.transpose(pp[tile_][0:TS, h // GH, (h % GH) * P:(h % GH + 1) * P], src(h), ident)
                    last.then_inc(s, 1)

                token_major(k_, 0, s3["ktr"])
                token_major(lambda h: qkv_s[:, h, 2, :], 1, s3["vtr"])
                pe.wait_ge(s_ld, 16 * H)
                pe.wait_ge(s3["egrow"], 1)
                pe.wait_ge(s3["dsub"], 1)
                for h in range(H):
                    for s in range(NSEQ):
                        t = slice(LS * s, LS * (s + 1))
                        last = nc.tensor.matmul(cols(0, h)[:, t], s_s[:, h, s, :], k_(h)[:, t], start=True, stop=True)
                last.then_inc(s3["ks"], 1)
                identh = cst[0:TS, CST["ident"][0]:CST["ident"][0] + TS]
                pe.wait_ge(s3["tu"], 1)
                for h in range(H):
                    last = nc.tensor.transpose(cols(2, h, TS), tu_s[:, h, :], identh)
                last.then_inc(s3["tr"], 1)
                pe.wait_ge(s3["ti"], 1)
                pe.wait_ge(s3["lm"], 1)
                for h in range(H):
                    last = nc.tensor.matmul(cols(1, h, TS), lm_s[:, h, :], ti_s[:, h, :], start=True, stop=True)
                last.then_inc(s3["a"], 1)
                pe.wait_ge(s3["ap"], 1)
                pe.wait_ge(s3["qkm"], 1)
                for h in range(H):
                    last = nc.tensor.matmul(cols(3, h, TS), ap_s[:, h, :], tu_s[:, h, :], start=True, stop=True)
                last.then_inc(s3["du"], 1)
                pe.wait_ge(s3["ksc"], 1)
                pe.wait_ge(s3["kt"], 1)
                token_major(lambda h: ks_s[:, h, :], 0, s3["kst"])
                pe.wait_ge(s3["r"], 1)
                pe.wait_ge(s3["tu"], 2)
                for h in range(H):
                    last = nc.tensor.matmul(pp[1][0:TS, h // GH, (h % GH) * P:(h % GH + 1) * P], tu_s[:, h, :],
                                            r_s[:, h, :], start=True, stop=True)
                last.then_inc(s3["vn"], 1)
                pe.wait_ge(s3["vnc"], 1)
                pe.wait_ge(s3["qe"], 1)
                for h in range(H):
                    nc.tensor.matmul(cols(0, h), vn_s[:, h, :], qk_s[:, h, :], start=True, stop=True,
                                     skip_group_check=True)
                    for s in range(NSEQ):
                        t = slice(LS * s, LS * (s + 1))
                        last = nc.tensor.matmul(cols(0, h)[:, t], s_s[:, h, s, :], qe_s[:, h, t], start=False,
                                                stop=True, skip_group_check=True)
                last.then_inc(s3["o"], 1)
                pe.wait_ge(s3["osq"], 1)
                nc.tensor.matmul(dd[:, 1, 0:H * TS], ones, osq_s[:].rearrange("p h t -> p (h t)"), start=True,
                                 stop=True).then_inc(s3["oss"], 1)
                for h in range(H):
                    pe.wait_ge(s3["km"], h + 1)
                    if h >= 2:
                        pe.wait_ge(s3["snew"], 2 * h - 2)
                    for s in range(NSEQ):
                        last = nc.tensor.matmul(pp[h % 2][:, s // GH, (s % GH) * P:(s % GH + 1) * P],
                                                km_s[h % 2][:, s, :], vn_s[:, h, :], start=True, stop=True)
                    last.then_inc(s3["ds"], 1)

            @block.scalar
            def _(act):
                a_ = Steps(act, s3["act"])
                act.wait_ge(s3["dsub"], 1)
                nc.scalar.activation(eg_s[:], dd[:, 0, 0:H * TS].rearrange("p (h t) -> p h t", h=H),
                                     ACT.Exp).then_inc(s3["egrow"], 1)
                act.wait_ge(s3["dsub"], 2)
                nc.scalar.activation(decay_s[:], decay_s[:], ACT.Exp).then_inc(s3["dexp"], 1)
                act.wait_ge(s3["ks"], 1)
                nc.scalar.activation(ks_s[:], dd[:, 0, 0:H * TS].rearrange("p (h t) -> p h t", h=H),
                                     ACT.Copy).then_inc(s3["ksc"], 1)
                act.wait_ge(s3["tr"], 1)
                nc.scalar.activation(ti_s[:], dd[0:TS, 2, 0:H * TS].rearrange("p (h t) -> p h t", h=H),
                                     ACT.Copy).then_inc(s3["ti"], 1)
                act.wait_ge(s3["a"], 1)
                nc.scalar.activation(ap_s[:], dd[0:TS, 1, 0:H * TS].rearrange("p (h t) -> p h t", h=H),
                                     ACT.Copy).then_inc(s3["ap"], 1)
                act.wait_ge(s3["vn"], 1)
                nc.scalar.activation(vn_s[:].rearrange("p (b h) n -> p b (h n)", b=2), pp[1][0:TS, :, :],
                                     ACT.Copy).then_inc(s3["vnc"], 1)
                act.wait_ge(s3["o"], 1)
                o = dd[:, 0, 0:H * TS].rearrange("p (h t) -> p h t", h=H)
                nc.scalar.activation(osq_s[:], o, ACT.Square).then_inc(s3["osq"], 1)
                act.wait_ge(s3["oss"], 1)
                a_(nc.scalar.activation(ors_s[:], dd[:, 1, 0:H * TS].rearrange("p (h t) -> p h t", h=H), ACT.Sqrt,
                                        bias=eps[:], scale=1.0 / P))
                a_.settle()
                act.sem_inc(s3["ors"], 1)

            @block.vector
            def _(dve):
                st = Steps(dve, s3["dve"])

                def heads(bank, rows=P):
                    return dd[0:rows, bank, 0:H * TS].rearrange("p (h t) -> p h t", h=H)

                def wide(t):
                    return t[0:TS].rearrange("p b (h n) -> p b h n", h=GH)

                def wide_sb(t):
                    return t[:].rearrange("p (b h) n -> p b h n", b=2)

                def wide_cols(a):
                    return a.rearrange("p (b h) -> p b h", b=2).unsqueeze(3).to_broadcast([TS, 2, GH, P])

                dve.wait_ge(s3["grow"], 1)
                nc.vector.tensor_tensor(decay_s[:], heads(0, TS), head_cols(tok[0:TS, GCUM, NC, :]),
                                        ALU.subtract).then_inc(s3["dsub"], 1)
                dve.wait_ge(s3["dsub"], 1)
                nc.vector.tensor_scalar(decay_s[:], decay_s[:], 0.0, None, ALU.min).then_inc(s3["dsub"], 1)
                dve.wait_ge(s3["brow"], 1)
                nc.vector.tensor_tensor(kb_s[:], qkv_s[:, :, 1, :], heads(1), ALU.mult).then_inc(s3["kb"], 1)
                dve.wait_ge(s3["egrow"], 1)
                nc.vector.tensor_tensor(qe_s[:], qkv_s[:, :, 0, :], eg_s[:], ALU.mult).then_inc(s3["qe"], 1)
                dve.wait_ge(s3["dexp"], 1)
                st(nc.vector.tensor_tensor(decay_s[:], decay_s[:], head_tile(c_("uts", TS)), ALU.mult))
                dve.wait_ge(s3["kk"], 1)
                st.settle()
                st(nc.vector.tensor_tensor(lt_s[:], heads(2, TS), decay_s[:], ALU.mult))
                dve.wait_ge(s3["qk"], 1)
                nc.vector.tensor_tensor(qk_s[:], heads(3, TS), decay_s[:], ALU.mult).then_inc(s3["qkm"], 1)
                st.settle()
                st(nc.vector.tensor_tensor(tu_s[:], lt_s[:], head_tile(level(0, TS)), ALU.mult))
                st.settle()
                nc.vector.tensor_tensor(tu_s[:], head_tile(cst[0:TS, CST["ident"][0]:CST["ident"][0] + TS]), tu_s[:],
                                        ALU.subtract).then_inc(s3["tu"], 1)
                nc.vector.tensor_tensor(lm_s[:], lt_s[:], head_tile(level(1, TS)), ALU.mult).then_inc(s3["lm"], 1)
                dve.wait_ge(s3["ktr"], 1)
                nc.vector.tensor_tensor(wide_sb(kt_s), wide(pp[0]), wide_cols(tok[0:TS, ETAIL, NC, :]),
                                        ALU.mult).then_inc(s3["kt"], 1)
                dve.wait_ge(s3["vtr"], 1)
                st(nc.vector.tensor_tensor(wide_sb(vb_s), wide(pp[1]), wide_cols(tok[0:TS, BETA, NC, :]), ALU.mult))
                dve.wait_ge(s3["du"], 1)
                dve.wait_ge(s3["tu"], 1)
                nc.vector.tensor_tensor(tu_s[:], tu_s[:], heads(3, TS), ALU.subtract).then_inc(s3["tu"], 1)
                dve.wait_ge(s3["kst"], 1)
                st(nc.vector.tensor_tensor(wide_sb(r_s), wide(pp[0]), wide_cols(tok[0:TS, NBEG, NC, :]), ALU.mult))
                st.settle()
                nc.vector.tensor_tensor(r_s[:], r_s[:], vb_s[:], ALU.add).then_inc(s3["r"], 1)
                dve.wait_ge(s3["kt"], 1)

                def masked_k(h):
                    nc.vector.tensor_tensor(km_s[h % 2][:], kt_s[:, h, :].unsqueeze(1).to_broadcast([TS, NSEQ, P]),
                                            c_("seqmask", TS).unsqueeze(2).to_broadcast([TS, NSEQ, P]),
                                            ALU.mult).then_inc(s3["km"], 1)

                masked_k(0)
                masked_k(1)
                dve.wait_ge(s3["ors"], 1)
                st(nc.vector.reciprocal(ors_s[:], ors_s[:]))
                st.settle()
                st(nc.vector.tensor_tensor(ors_s[:], heads(0), ors_s[:], ALU.mult))
                st.settle()
                st(nc.vector.scalar_tensor_tensor(out=ors_s[:], in0=ors_s[:], scalar=v_("dn_g"), in1=zg[:, :, TP:NT],
                                                  op0=ALU.mult, op1=ALU.mult))
                st.settle()
                nc.vector.tensor_tensor(mixed[:, :, TP:NT], mixed[:, :, TP:NT], ors_s[:], ALU.add).then_inc(s3["mix"], 1)
                for h in range(H):
                    last_g = eg_s[:, h, :].rearrange("p (s t) -> p s t", s=NSEQ)[:, :, LS - 1:LS].to_broadcast([P, NSEQ, P])
                    dve.wait_ge(s3["o"], 1)
                    nc.vector.tensor_tensor(s_s[:, h], s_s[:, h], last_g, ALU.mult).then_inc(s3["snew"], 1)
                    dve.wait_ge(s3["snew"], 2 * h + 1)
                    dve.wait_ge(s3["ds"], h + 1)
                    new = s_s[:, h].rearrange("p (b s) n -> p b (s n)", b=2)
                    nc.vector.tensor_tensor(new, new, pp[h % 2][:], ALU.add).then_inc(s3["snew"], 1)
                    if h + 2 < H:
                        masked_k(h + 2)
                dve.wait_ge(s3["mix"], 1)

        mix_hi_done, mix_lo_done, res_done = sem("mix_hi_done"), sem("mix_lo_done"), sem("res_done")
        sq2_done, ss2_done, rt2_done, h2_done, h2_hi_done, h2_lo_done, p4_dve = (
            sem("sq2_done"), sem("ss2_done"), sem("rt2_done"), sem("h2_done"), sem("h2_hi_done"), sem("h2_lo_done"),
            sem("p4_dve"))

        def add_gated(dve, st, xs, src0, src1, gate_p, gate_s, tmp, last_inc):
            st(nc.vector.scalar_tensor_tensor(out=xs[:, 0:HN], in0=src0, scalar=gate_p, in1=xs[:, 0:HN],
                                              op0=ALU.mult, op1=ALU.add))
            st(nc.vector.scalar_tensor_tensor(out=xs[:, HN:TP], in0=src1[:, 0:TP - HN], scalar=gate_p,
                                              in1=xs[:, HN:TP], op0=ALU.mult, op1=ALU.add))
            seq = "p (s t) -> p s t"
            ins = nc.vector.tensor_tensor(tmp.rearrange(seq, s=NSEQ), src1[:, TP - HN:HN].rearrange(seq, s=NSEQ),
                                          gate_s, ALU.mult)
            if last_inc is not None:
                ins.then_inc(last_inc, 1)
            else:
                st(ins)

        ended, now = now, list(phase_sems)
        phase_sems.clear()
        with nc.Block() as block:
            @block.gpsimd
            def _(pool):
                retire(pool, ended)

            @block.sync
            def _(sp):
                with sp.Fori(0, KC // 2) as i:
                    for o in range(2):
                        load_chunk(sp, Chunk(C_OUT + 2, o, 2, i))

            @block.tensor
            def _(pe):
                pe.wait_ge(mix_lo_done, 1)
                with pe.Fori(0, KC // 2) as i:
                    for o in range(2):
                        product(pe, Chunk(C_OUT, o, 2, i))
                for k in range(KC):
                    pe.wait_ge(sq2_done, k + 1)
                    for b in range(2):
                        last = nc.tensor.matmul(dd[:, b, 0:HN], ones, sq2[:, k, b * HN:(b + 1) * HN],
                                                start=(k == 0), stop=(k == KC - 1))
                last.then_inc(ss2_done, 1)

            @block.scalar
            def _(act):
                hi_act(act, mixed, mix_hi_done)
                with act.Fori(0, KC // 2) as i:
                    for o in range(2):
                        split_hi(act, Chunk(C_OUT, o, 2, i) + 1)
                for k in range(KC):
                    act.wait_ge(res_done, k + 1)
                    nc.scalar.activation(sq2[:, k, :], x[:, k, :], ACT.Square).then_inc(sq2_done, 1)
                act.wait_ge(ss2_done, 1)
                nc.scalar.activation(halves(rstd2[:]), dd[:, 0:2, 0:HN], ACT.Sqrt, bias=eps[:],
                                     scale=1.0 / D).then_inc(rt2_done, 1)
                act.wait_ge(h2_done, 1)
                hi_act(act, h2, h2_hi_done)

            @block.vector
            def _(dve):
                split_act(dve, mixed, mix_hi_done, mix_lo_done)
                n_own = 2
                with dve.Fori(0, KC // 2) as i:
                    for o in range(2):
                        k = Chunk(C_OUT, o, 2, i)
                        m = 2 * i + o
                        st = Steps(dve, p4_dve, n_own * m)
                        split_lo(dve, k + 1)
                        gate_dve(dve, pp_done[k.slot], k.turn + 2)
                        xs = x[:, bass.ds(m, 1), :].rearrange("p a n -> p (a n)")
                        g_p = mod[:, bass.ds(m + G1, 1), 0:1].rearrange("p a n -> p (a n)")
                        g_s = mod[:, bass.ds(m + G1, 1), 1:NG].rearrange("p a n -> p (a n)").unsqueeze(2).to_broadcast(
                            [P, NSEQ, LS])
                        add_gated(dve, st, xs, pp[k.slot][:, 0, 0:HN], pp[k.slot][:, 1, 0:HN], g_p, g_s, res_t[o][:],
                                  pp_read[k.slot])
                        gate_dve(dve, pp_read[k.slot], k.turn + 2)
                        nc.vector.tensor_tensor(xs[:, TP:NT], xs[:, TP:NT], res_t[o][:], ALU.add).then_inc(res_done, 1)
                        assert st.n == n_own
                st = Steps(dve, p4_dve, n_own * KC)
                dve.wait_ge(rt2_done, 1)
                st(nc.vector.reciprocal(rstd2[:], rstd2[:]))
                st.settle()
                norm_affine(dve, st, h2, x, rstd2, aff2, SH2, h2_done)
                split_act(dve, h2, h2_hi_done, h2_lo_done)
                dve.wait_ge(h2_lo_done, 1)

        keys_ld, sc_done, sc_read, sc_zero = sem("keys_ld"), sem("sc_done"), sem("sc_read"), sem("sc_zero")
        ended, now = now, list(phase_sems)
        phase_sems.clear()
        with nc.Block() as block:
            @block.gpsimd
            def _(pool):
                retire(pool, ended)

            @block.sync
            def _(sp):
                sp.dma_start(keys[:], keys_in).then_inc(keys_ld, 16)
                with sp.Fori(0, H) as i:
                    for o in range(2):
                        load_chunk(sp, Chunk(C_QUERY + 2, o, 2, i))

            @block.tensor
            def _(pe):
                def score(i, o):
                    k = Chunk(C_QUERY, o, 2, i)
                    read(pe, k)
                    pe.wait_ge(sc_read, 2 * i + o + 1)
                    for t in range(TT):
                        m = P if t < NC else TS
                        last = nc.tensor.matmul(dd[0:m, 2 * o + t // NC, (t % NC) * P:(t % NC + 1) * P],
                                                qt[k.slot][:, t * P:t * P + m],
                                                keys[:, bass.ds(2 * i + o, 1), :].rearrange("p a n -> p (a n)"),
                                                start=True, stop=True)
                    last.then_inc(sc_done, 1)

                pe.wait_ge(keys_ld, 16)
                with pe.Fori(0, H) as i:
                    for o in range(2):
                        product(pe, Chunk(C_QUERY, o, 2, i))
                    for o in range(2):
                        score(i, o)

            @block.scalar
            def _(act):
                with act.Fori(0, H) as i:
                    for o in range(2):
                        k = Chunk(C_QUERY, o, 2, i)
                        split_hi(act, k + 1)
                        done(act, k)
                        act.wait_ge(sc_read, 2 * i + o + 1)
                        nc.scalar.activation(halves(qt[k.slot][:]), pp[k.slot][:, :, 0:HN],
                                             ACT.Copy).then_inc(pp_read[k.slot], 1)

            @block.vector
            def _(dve):
                dve.sem_inc(sc_read, 2)
                nc.vector.memset(scores[:, NC], 0.0).then_inc(sc_zero, 1)
                dve.wait_ge(sc_zero, 1)
                with dve.Fori(0, H) as i:
                    for o in range(2):
                        split_lo(dve, Chunk(C_QUERY, o, 2, i) + 1)
                    for o in range(2):
                        gate_dve(dve, sc_done, 2 * i + o + 1)
                        col = scores[:, :, bass.ds(2 * i + o, 1), :].rearrange("p t a n -> p t (a n)")
                        nc.vector.tensor_copy(col[:, 0:NC, :], dd[:, 2 * o, :].rearrange("p (t n) -> p t n", t=NC))
                        nc.vector.tensor_copy(col[0:TS, NC, :], dd[0:TS, 2 * o + 1, 0:P]).then_inc(sc_read, 1)
                dve.wait_ge(sc_read, 2 + 2 * H)

        wk_ready, wk_used, p5_dve, ex_in, ex_out, trio_ready, trio_tr = (
            sem("wk_ready"), sem("wk_used"), sem("p5_dve"), sem("ex_in"), sem("ex_out"), sem("trio_ready"),
            sem("trio_tr"))
        gcols_ready, hot_a_ready, hot_b_ready, quad_done, quad_read = (
            sem("gcols_ready"), sem("hot_a_ready"), sem("hot_b_ready"), sem("quad_done"), sem("quad_read"))
        gates_st = [sem(f"gates_st{s}") for s in range(2)]
        LOWEST = -3.0e38
        NQ = TB // 4
        TQ = P // 4

        ended, now = now, list(phase_sems)
        phase_sems.clear()
        with nc.Block() as block:
            @block.scalar
            def _(act):
                act.sem_inc(quad_read, 4)
                for s in range(2):
                    act.sem_inc(gates_st[s], 16)

                def evac(u, n):
                    for q in range(n // 4):
                        s, b = (q // NQ) % 2, q // NQ
                        if q % NQ == 0:
                            act.wait_ge(gates_st[s], u * 32 + (16 * (b // 2) + 16))
                        act.wait_ge(quad_done, u * TQ + (q + HOTS + 1))
                        out = gstage[s][:, :, 4 * (q % NQ):4 * (q % NQ) + 4].rearrange("p j t -> p t j")
                        nc.scalar.activation(out, dd[:, q % 4, :].rearrange("p (t j) -> p t j", t=4),
                                             ACT.Copy).then_inc(quad_read, 1)

                def choice(t, beside):
                    gate_act(act, wk_used, t + 1)
                    nc.scalar.activation(wk[:].unsqueeze(1), scores[:, bass.ds(t, 1), :, :],
                                         ACT.Copy).then_inc(wk_ready, 1)
                    beside()
                    act.wait_ge(ex_in, t + 1)
                    nc.scalar.activation(best[:], best[:], ACT.Exp).then_inc(ex_out, 1)

                choice(0, lambda: None)
                with act.Fori(1, TT) as t:
                    choice(t, lambda: evac(t - 1, P))
                evac(TT - 1, TS)

            @block.tensor
            def _(pe):
                def quads(u, n):
                    for q in range(n // 4):
                        pe.wait_ge(hot_a_ready, u * TQ + (q + 1))
                        pe.wait_ge(hot_b_ready, u * TQ + (q + 1))
                        pe.wait_ge(quad_read, u * TQ + (q + 1))
                        for o in range(4):
                            v = (q % HOTS) * 4 + o
                            last = nc.tensor.matmul(dd[:, q % 4, o * P:(o + 1) * P], hot_a[:, v, :], hot_b[:, v, :],
                                                    start=True, stop=True)
                        last.then_inc(quad_done, 1)

                def turn(t):
                    pe.wait_ge(trio_ready, t + 1)
                    pe.wait_ge(gcols_ready, t + 1)
                    for n in range(3):
                        last = nc.tensor.transpose(pp[0][:, 0, n * P:(n + 1) * P], trio[:, n, :], ident)
                    last.then_inc(trio_tr, 1)

                pe.sem_inc(gcols_ready, 1)
                turn(0)
                with pe.Fori(1, TT) as t:
                    quads(t - 1, P)
                    turn(t)
                quads(TT - 1, TS)

            @block.gpsimd
            def _(pool):
                retire(pool, ended)

                def hots(u, n):
                    gate_pool(pool, gcols_ready, u + 2)
                    for q in range(n // 4):
                        gate_pool(pool, quad_done, u * TQ + (q + 1))
                        for o in range(4):
                            c = 4 * q + o
                            last = nc.gpsimd.tensor_scalar(hot_b[:, (q % HOTS) * 4 + o, :], iota, gcols[:, 1, c:c + 1],
                                                           None, ALU.is_equal)
                        last.then_inc(hot_b_ready, 1)

                with pool.Fori(0, TT - 1) as u:
                    hots(u, P)
                hots(TT - 1, TS)

            @block.vector
            def _(dve):
                dve.sem_inc(wk_used, 1)
                dve.sem_inc(trio_tr, 1)
                dve.sem_inc(quad_done, HOTS)
                n_own = 5 * 2 * H + 1 + 5 * H + 5 + 6 + 2

                def take(u):
                    gate_dve(dve, quad_done, u * TQ + HOTS)
                    gate_dve(dve, trio_tr, u + 2)
                    nc.vector.tensor_copy(gcols[:], pp[0][:, 0, 0:3 * P].rearrange("p (n t) -> p n t", n=3)).then_inc(gcols_ready, 1)
                    dve.wait_ge(gcols_ready, u + 2)

                def hot(u, q):
                    dve.wait_ge(quad_done, u * TQ + (q + 1))
                    for o in range(4):
                        c = 4 * q + o
                        last = nc.vector.tensor_scalar(hot_a[:, (q % HOTS) * 4 + o, :], iota, gcols[:, 0, c:c + 1],
                                                       gcols[:, 2, c:c + 1], ALU.is_equal, ALU.mult)
                    last.then_inc(hot_a_ready, 1)

                def top16(st, src, spare, values, index, n, beside):
                    for j in range(n):
                        st(nc.vector.max(values(j)[:, 0:8], src(j)))
                        if j % 4 == 1:
                            beside()
                    gate_dve(dve, p5_dve, st.before + st.n)
                    for j in range(n):
                        st(nc.vector.max_index(index(j)[:, 0:8], values(j)[:, 0:8], src(j)))
                        st(nc.vector.match_replace(spare(j), values(j)[:, 0:8], src(j), LOWEST))
                        if j % 2 == 1:
                            beside()
                    gate_dve(dve, p5_dve, st.before + st.n)
                    for j in range(n):
                        st(nc.vector.max(values(j)[:, 8:16], spare(j)))
                        if j % 4 == 1:
                            beside()
                    gate_dve(dve, p5_dve, st.before + st.n)
                    for j in range(n):
                        st(nc.vector.max_index(index(j)[:, 8:16], values(j)[:, 8:16], spare(j)))
                        if j % 4 == 1:
                            beside()
                    gate_dve(dve, p5_dve, st.before + st.n)

                def choice(t, beside):
                    st = Steps(dve, p5_dve, n_own * t)
                    gate_dve(dve, wk_ready, t + 1)
                    top16(st, lambda j: wk[:, j, :], lambda j: wk2[:, j, :], lambda j: top[:, j, :],
                          lambda j: top_i[:, j, :], 2 * H, beside)
                    dve.sem_inc(wk_used, 1)
                    pair = top[:].rearrange("p (h q) k -> p h q k", q=2)
                    a = pair[:, :, 0, :].unsqueeze(3).to_broadcast([P, H, TOPK, TOPK])
                    b = pair[:, :, 1, :].unsqueeze(2).to_broadcast([P, H, TOPK, TOPK])
                    st(nc.vector.tensor_tensor(cand[:], a, b, ALU.add))
                    beside()
                    gate_dve(dve, p5_dve, st.before + st.n)
                    flat = cand[:].rearrange("p h a b -> p h (a b)")
                    spare = wk2[:].rearrange("p (h q) k -> p h (q k)", q=2)
                    top16(st, lambda j: flat[:, j, :], lambda j: spare[:, j, :], lambda j: best[:, j, :],
                          lambda j: sel[:, j, :], H, beside)
                    st(nc.vector.tensor_copy(gsum[:].unsqueeze(2), best[:, :, 0:1]))
                    st.settle()
                    nc.vector.tensor_tensor(best[:], best[:], gsum[:].unsqueeze(2).to_broadcast([P, H, TOPK]),
                                            ALU.subtract).then_inc(ex_in, 1)
                    st(nc.vector.tensor_scalar(sel_ab[:, 0], sel[:], 4, None, ALU.logical_shift_right))
                    st(nc.vector.tensor_scalar(sel_ab[:, 1], sel[:], 15, None, ALU.bitwise_and))
                    st(nc.vector.tensor_copy(top_f[:], top_i[:]))
                    st.settle()
                    st(nc.vector.tensor_copy(sel_f[:], sel_ab[:]))
                    beside()
                    st.settle()
                    keys_of = top_f[:].rearrange("p (h q) k -> p h q k", q=2)
                    i16 = c_("iota16").unsqueeze(1).unsqueeze(1).to_broadcast([P, H, TOPK, TOPK])
                    for q in range(2):
                        if q == 0:
                            dve.wait_ge(trio_tr, t + 1)
                        st(nc.vector.tensor_tensor(cand[:], sel_f[:, q].unsqueeze(3).to_broadcast([P, H, TOPK, TOPK]), i16,
                                                   ALU.is_equal))
                        beside()
                        st.settle()
                        st(nc.vector.tensor_tensor(cand[:], cand[:],
                                                   keys_of[:, :, q, :].unsqueeze(2).to_broadcast([P, H, TOPK, TOPK]),
                                                   ALU.mult))
                        beside()
                        st.settle()
                        st(nc.vector.tensor_reduce(trio[:, q, :].rearrange("p (h k) -> p h k", h=H), cand[:], AX_X, ALU.add))
                        beside()
                        st.settle()
                    dve.wait_ge(ex_out, t + 1)
                    st(nc.vector.tensor_reduce(gsum[:], best[:], AX_X, ALU.add))
                    st.settle()
                    st(nc.vector.reciprocal(gsum[:], gsum[:]))
                    st.settle()
                    nc.vector.tensor_tensor(trio[:, 2, :].rearrange("p (h k) -> p h k", h=H), best[:],
                                            gsum[:].unsqueeze(2).to_broadcast([P, H, TOPK]), ALU.mult).then_inc(trio_ready, 1)
                    dve.wait_ge(trio_ready, t + 1)
                    assert st.n == n_own, st.n

                choice(0, lambda: None)
                with dve.Fori(1, TT) as t:
                    take(t - 1)
                    places = [0]

                    def beside():
                        places[0] += 1
                        if 2 < places[0] <= 2 + TQ:
                            hot(t - 1, places[0] - 3)

                    choice(t, beside)
                    assert places[0] >= 2 + TQ, places
                take(TT - 1)
                for q in range(TS // 4):
                    hot(TT - 1, q)

            @block.sync
            def _(sp):
                def store(u, n):
                    for b in range(n // TB):
                        sp.wait_ge(quad_read, u * TQ + (NQ * (b + 1) + 4))
                        sp.dma_start(gates_d[bass.ds(u * (P // TB) + b, 1)].rearrange("a i j t -> i a (j t)"),
                                     gstage[b % 2][:].rearrange("p j t -> p (j t)").unsqueeze(1)).then_inc(
                                         gates_st[b % 2], 16)

                with sp.Fori(0, TT - 1) as u:
                    store(u, P)
                store(TT - 1, TS)
                for s in range(2):
                    sp.wait_ge(gates_st[s], 16 * (1 + (NTB + 1 - s) // 2))

        v_landed = [sem(f"v_landed{s}") for s in range(2)]
        gt_landed, v_hi_done, v_lo_done, cf_done, c_hi_done, c_lo_done, po_done, acc_done, acc_zero = (
            sem("gt_landed"), sem("v_hi_done"), sem("v_lo_done"), sem("cf_done"), sem("c_hi_done"), sem("c_lo_done"),
            sem("po_done"), sem("acc_done"), sem("acc_zero"))

        def groups(eng, body):
            with eng.Fori(0, NGRP - 1) as g:
                body(g, lambda off: Chunk(C_U, off, JG, g), False)
            body(NGRP - 1, lambda off: Chunk(C_U + JG * (NGRP - 1), off), True)

        ended, now = now, list(phase_sems)
        phase_sems.clear()
        with nc.Block() as block:
            @block.gpsimd
            def _(pool):
                retire(pool, ended)

            @block.sync
            def _(sp):
                def load_v(s, idx):
                    sp.dma_start(v_raw[s][:].unsqueeze(1), v_in[bass.ds(idx, 1)].rearrange(
                        "a p n -> p a n")).then_inc(v_landed[s], 16)

                def load_gates(g):
                    sp.dma_start(gt[:].rearrange("p b j t -> p b (j t)"),
                                 gates_d[:, :, bass.ds(g * JG, JG), :].rearrange(
                                     "b i j t -> i b (j t)")).then_inc(gt_landed, 16)

                load_gates(0)
                load_v(0, 0)
                load_v(1, 1)
                load_chunk(sp, Chunk(C_U + 2))
                load_chunk(sp, Chunk(C_U + 3))

                def body(g, chunk, tail):
                    for w in range(JG):
                        if not tail:
                            load_chunk(sp, chunk(w + 4))
                        if not tail or w < 2:
                            sp.wait_ge(v_lo_done, JG * g + w + 1)
                            load_v(w % 2, JG * g + w + 2)
                    if not tail:
                        sp.wait_ge(cf_done, JG * g + JG)
                        load_gates(g + 1)

                groups(sp, body)

            @block.tensor
            def _(pe):
                pe.sem_inc(po_done, 1)
                product(pe, Chunk(C_U))

                def body(g, chunk, tail):
                    for w in range(JG if not tail else JG - 1):
                        product(pe, chunk(w + 1))
                    pe.wait_ge(v_lo_done, JG * g + JG)
                    pe.wait_ge(c_lo_done, JG * g + JG)
                    for d in range(KC):
                        pe.wait_ge(acc_done, KC * g + d + 1)
                        for j in range(JG):
                            for w, a in ((v_hi[j], co_hi[j]), (v_hi[j], co_lo[j]), (v_lo[j], co_hi[j])):
                                for b in range(2):
                                    last = nc.tensor.matmul(
                                        dd[:, 2 * (d % 2) + b, 0:HN], w[:, d * P:(d + 1) * P],
                                        a[:, b * HN:(b + 1) * HN],
                                        start=(j == 0 and w is v_hi[0] and a is co_hi[0]),
                                        stop=(j == JG - 1 and w is v_lo[j]))
                        last.then_inc(po_done, 1)

                groups(pe, body)

            @block.scalar
            def _(act):
                def gelu(k):
                    done(act, k)
                    nc.scalar.activation(halves(ge[k.slot][:]), pp[k.slot][:, :, 0:HN], ACT.Gelu).then_inc(
                        pp_read[k.slot], 1)

                split_hi(act, Chunk(C_U + 1))
                gelu(Chunk(C_U))

                def body(g, chunk, tail):
                    for w in range(JG):
                        if not tail or w < 2:
                            split_hi(act, chunk(w + 2))
                        act.wait_ge(v_landed[w % 2], g * 32 + (16 * (w // 2) + 16))
                        act.wait_ge(po_done, KC * g + 1)
                        nc.scalar.activation(v_hi[w][:], v_raw[w % 2][:], ACT.Copy).then_inc(v_hi_done, 1)
                        act.wait_ge(cf_done, JG * g + w + 1)
                        nc.scalar.activation(co_hi[w][:], cf[w % 2][:], ACT.Copy).then_inc(c_hi_done, 1)
                        if not tail or w < 3:
                            gelu(chunk(w + 1))

                groups(act, body)

            @block.vector
            def _(dve):
                dve.sem_inc(acc_done, 2)
                nc.vector.memset(acc[:], 0.0).then_inc(acc_zero, 1)
                dve.wait_ge(acc_zero, 1)
                split_lo(dve, Chunk(C_U + 1))

                def body(g, chunk, tail):
                    for w in range(JG):
                        read(dve, chunk(w))
                        dve.wait_ge(gt_landed, 16 * g + 16)
                        nc.vector.tensor_tensor(cf[w % 2][:].rearrange("p (b t) -> p b t", t=TB),
                                                ge[w % 2][:].rearrange("p (b t) -> p b t", t=TB), gt[:, :, w, :],
                                                ALU.mult).then_inc(cf_done, 1)
                        if not tail or w < 2:
                            split_lo(dve, chunk(w + 2))
                        dve.wait_ge(v_hi_done, JG * g + w + 1)
                        nc.vector.tensor_tensor(v_lo[w][:], v_raw[w % 2][:], v_hi[w][:].bitcast(F32),
                                                ALU.subtract).then_inc(v_lo_done, 1)
                        dve.wait_ge(c_hi_done, JG * g + w + 1)
                        nc.vector.tensor_tensor(co_lo[w][:], cf[w % 2][:], co_hi[w][:].bitcast(F32),
                                                ALU.subtract).then_inc(c_lo_done, 1)
                    for d in range(KC):
                        dve.wait_ge(po_done, KC * g + d + 2)
                        o = halves(acc[:, d, :])
                        nc.vector.tensor_tensor(o, o, dd[:, 2 * (d % 2):2 * (d % 2) + 2, 0:HN],
                                                ALU.add).then_inc(acc_done, 1)

                groups(dve, body)
                dve.wait_ge(acc_done, 2 + KC * NGRP)

        p8_dve, x3_done, sq3_done, ss3_done, rt3_done, y_done = (
            sem("p8_dve"), sem("x3_done"), sem("sq3_done"), sem("ss3_done"), sem("rt3_done"), sem("y_done"))
        ended, now = now, list(phase_sems)
        phase_sems.clear()
        with nc.Block() as block:
            @block.gpsimd
            def _(pool):
                retire(pool, ended)

            @block.vector
            def _(dve):
                st = Steps(dve, p8_dve)
                for k in range(KC):
                    st(nc.vector.scalar_tensor_tensor(out=x[:, k, 0:TP], in0=acc[:, k, 0:TP],
                                                      scalar=mod[:, G2 + k, 0:1], in1=x[:, k, 0:TP],
                                                      op0=ALU.mult, op1=ALU.add))
                g_s = mod[:, G2:G2 + KC, 1:NG].unsqueeze(3).to_broadcast([P, KC, NSEQ, LS])
                st(nc.vector.tensor_tensor(sample_cols(acc), sample_cols(acc), g_s, ALU.mult))
                st.settle()
                nc.vector.tensor_tensor(x[:, :, TP:NT], x[:, :, TP:NT], acc[:, :, TP:NT], ALU.add).then_inc(x3_done, 1)
                dve.wait_ge(x3_done, 1)
                dve.wait_ge(rt3_done, 1)
                st(nc.vector.reciprocal(rstd3[:], rstd3[:]))
                st.settle()
                for k in range(KC):
                    nc.vector.scalar_tensor_tensor(out=acc[:, k, :], in0=x[:, k, :],
                                                   scalar=vec[:, VEC["gf"][0] + k:VEC["gf"][0] + k + 1],
                                                   in1=rstd3[:], op0=ALU.mult, op1=ALU.mult).then_inc(y_done, 1)

            @block.scalar
            def _(act):
                act.wait_ge(x3_done, 1)
                for k in range(KC):
                    nc.scalar.activation(sq3[:, k, :], x[:, k, :], ACT.Square).then_inc(sq3_done, 1)
                act.wait_ge(ss3_done, 1)
                nc.scalar.activation(halves(rstd3[:]), dd[:, 0:2, 0:HN], ACT.Sqrt, bias=eps[:],
                                     scale=1.0 / D).then_inc(rt3_done, 1)

            @block.tensor
            def _(pe):
                for k in range(KC):
                    pe.wait_ge(sq3_done, k + 1)
                    for b in range(2):
                        last = nc.tensor.matmul(dd[:, b, 0:HN], ones, sq3[:, k, b * HN:(b + 1) * HN],
                                                start=(k == 0), stop=(k == KC - 1))
                last.then_inc(ss3_done, 1)

            @block.sync
            def _(sp):
                for k in range(0, KC, 4):
                    sp.wait_ge(y_done, k + 4)
                    sp.dma_start(y_out[:, k:k + 4, :], acc[:, k:k + 4, :]).then_inc(out_st, 16)
                    n_out[0] += 1
                sp.wait_ge(out_st, 16 * n_out[0])


OUTPUTS = (("y", (P, KC, NT)), ("conv", (P, 3 * H, NG, CW - 1)), ("delta_p", (P, H, P)),
           ("delta_s", (H, P, NSEQ, P)), ("pool", (P, len(WINDOWS), NG, PB_)))


def layout(i):
    def rows(a, n):
        return a.reshape(KC, P, n, P).transpose(2, 1, 0, 3).reshape(n, P, D)

    def per_feature(a):
        return a.reshape(-1, P).T

    i = {k: np.asarray(v) for k, v in i.items()}
    w_in = i["w_in"][0]
    qkv_w = 3 * D
    z0 = qkv_w + 2 * H
    pool0, ga0 = z0 + D, z0 + D + 4 * P
    gb0 = ga0 + D
    qkv = rows(w_in[:, :qkv_w], 3 * H).reshape(3, H, P, D).transpose(1, 0, 2, 3).reshape(3 * H, P, D)
    u = i["expert_u"][0].reshape(NEXP, NEXP, KC, P).transpose(1, 3, 2, 0).reshape(NEXP, P, D)
    stream = np.concatenate([
        rows(w_in[:, z0:z0 + D], N_Z), rows(w_in[:, ga0:ga0 + D], N_GA), rows(w_in[:, pool0:pool0 + 4 * P], N_POOL),
        rows(w_in[:, gb0:gb0 + D], N_GB), qkv, rows(i["w_out"][0], KC), rows(i["w_query"][0], 2 * H), u])
    conv_w = i["conv_w"][0].reshape(CW, 3, H, P).transpose(3, 2, 1, 0).reshape(P, 3 * H * CW)
    vec = np.concatenate([
        per_feature(i["norm1_g"][0]), per_feature(i["norm2_g"][0]), per_feature(i["final_norm_g"]),
        per_feature(i["pool_scale"][0]), per_feature(i["b_ada"][0]), per_feature(i["dn_norm_g"][0]), conv_w,
        np.tile(i["dt_bias"][0], (P, 1)), np.tile(i["a_log"][0], (P, 1))], 1)
    x = np.concatenate([i["x_prompt"][0], i["x_sample"].reshape(TS, D)]).T
    c = np.concatenate([i["c_prompt"], i["c_sample"]]).T
    ada = i["w_ada"][0].reshape(KC, P, N_ADA, 4 * P).transpose(2, 1, 0, 3)
    return {
        "x": x.reshape(KC, P, NT).transpose(1, 0, 2),
        "c": c.reshape(KC, P, NG).transpose(1, 0, 2),
        "vec": vec,
        "cst": constants(),
        "wba": w_in[:, qkv_w:z0].reshape(KC, P, 2 * H).transpose(1, 0, 2),
        "ada": ada,
        "stream": stream,
        "v": i["expert_v"][0].reshape(NEXP, NEXP, D).transpose(1, 0, 2),
        "conv": i["state_conv"][0].reshape(NSEQ, CW - 1, 3, H, P).transpose(4, 3, 2, 0, 1).reshape(P, 3 * H, NSEQ, CW - 1),
        "pool": i["state_pool"][0].reshape(NSEQ, PB_, len(WINDOWS), P).transpose(3, 2, 0, 1),
        "delta": i["state_delta"][0].transpose(1, 2, 0, 3),
        "wpool": i["w_pool"][0].transpose(1, 0, 2),
        "keys": i["sub_keys"][0].reshape(2 * H, NEXP, P).transpose(2, 0, 1),
    }


def kernel(**inputs):
    import concourse.bacc as bacc
    from concourse.bass_utils import run_bass_kernel_spmd

    nc = bacc.Bacc("TRN2", target_bir_lowering=False, num_devices=1)
    arrays, args = {}, []
    for name, a in layout(inputs).items():
        a = np.ascontiguousarray(a)
        arrays[f"in_{name}"] = a
        args.append(nc.dram_tensor(f"in_{name}", a.shape, mybir.dt.from_np(a.dtype), kind="ExternalInput").ap())
    for name, shape in OUTPUTS:
        args.append(nc.dram_tensor(f"out_{name}", shape, F32, kind="ExternalOutput").ap())
    build(nc, *args)
    r = run_bass_kernel_spmd(nc, [arrays], core_ids=[0]).results[0]
    y = r["out_y"].transpose(2, 1, 0).reshape(NT, D)
    conv = r["out_conv"].reshape(P, H, 3, NG, CW - 1).transpose(3, 4, 2, 1, 0).reshape(NG, CW - 1, 3 * D)
    pool = r["out_pool"].transpose(2, 3, 1, 0).reshape(NG, PB_, 4 * P)
    delta_p = r["out_delta_p"].transpose(1, 0, 2)
    delta_s = r["out_delta_s"].transpose(2, 0, 1, 3)
    return (y[None, :TP], y[TP:].reshape(NSEQ, LS, D), conv[None, :1], delta_p[None, None], pool[None, :1],
            conv[None, 1:], delta_s[None], pool[None, 1:])
```
